# Optimizing a Trainium2 kernel written in Bass

```python
import math
import jax, jax.numpy as jnp
from jax import lax
import numpy as np

D_MODEL = 2048
BATCH = 1
SEQ = 512
DEPTH = 1

CHUNK = 64
MIX_WIDTH = D_MODEL
RET_WIDTH = MIX_WIDTH // 2
LRU_WIDTH = MIX_WIDTH - RET_WIDTH
RET_HEADS = 8
RET_HEAD_DIM = RET_WIDTH // RET_HEADS
LRU_BLOCKS = 8
LRU_BLOCK_DIM = LRU_WIDTH // LRU_BLOCKS
CONV_WIDTH = 4
LRU_C = 8.0
ROPE_BASE = 10000.0
PEER_HEADS = 8
PEER_QUERY_DIM = 256
PEER_HALF = PEER_QUERY_DIM // 2
N_KEYS = 128
N_EXPERTS = N_KEYS * N_KEYS
PEER_TOPK = 16
PEER_TOKEN_BLOCK = 128
IN_COLS = 4 * RET_WIDTH + 2 * LRU_WIDTH
DN_ALPHA = (2.0 * DEPTH) ** 0.25
DN_BETA = (8.0 * DEPTH) ** -0.25
LN_EPS = 1e-5
GN_EPS = 1e-6

kernel_name = "hybrid_retention_rglru_peer_deepnorm"

def layer_norm(x, g, b):
    x32 = x.astype(jnp.float32)
    mu = jnp.mean(x32, axis=-1, keepdims=True)
    var = jnp.mean(jnp.square(x32 - mu), axis=-1, keepdims=True)
    return (x32 - mu) * lax.rsqrt(var + LN_EPS) * g + b

def rotary(x, positions):
    half = x.shape[-1] // 2
    inv_freq = ROPE_BASE ** (-jnp.arange(half, dtype=jnp.float32) / half)
    ang = positions.astype(jnp.float32)[..., None] * inv_freq
    cos = jnp.cos(ang)[:, :, None, :]
    sin = jnp.sin(ang)[:, :, None, :]
    x1, x2 = x[..., :half], x[..., half:]
    return jnp.concatenate([x1 * cos - x2 * sin, x2 * cos + x1 * sin], axis=-1)

def retention(q, k, v, g, positions):
    B, S = q.shape[:2]
    NC = S // CHUNK
    H, dh = RET_HEADS, RET_HEAD_DIM
    q = rotary(q.reshape(B, S, H, dh).astype(jnp.float32), positions) * (dh ** -0.5)
    k = rotary(k.reshape(B, S, H, dh).astype(jnp.float32), positions)
    v = v.reshape(B, S, H, dh).astype(jnp.float32)
    gamma = 1.0 - 2.0 ** (-5.0 - jnp.arange(H, dtype=jnp.float32))
    log_g = jnp.log(gamma)
    l = jnp.arange(CHUNK, dtype=jnp.float32)
    d_intra = jnp.exp(log_g[:, None, None] * jnp.abs(l[:, None] - l[None, :]))
    q_dec = jnp.exp(log_g[None, :] * (l[:, None] + 1.0))
    k_dec = jnp.exp(log_g[None, :] * (CHUNK - 1.0 - l[:, None]))
    chunk_dec = jnp.exp(log_g * CHUNK)
    qc = q.reshape(B, NC, CHUNK, H, dh)
    kc = k.reshape(B, NC, CHUNK, H, dh)
    vc = v.reshape(B, NC, CHUNK, H, dh)
    scores = jnp.einsum('bncht,bnmht->bnhcm', qc, kc) * d_intra
    o_intra = jnp.einsum('bnhcm,bnmhe->bnche', scores, vc)
    kv = jnp.einsum('bnmht,bnmhe->bnhte', kc * k_dec[:, :, None], vc)

    def step(state, kv_n):
        return chunk_dec[:, None, None] * state + kv_n, state

    _, states = lax.scan(step, jnp.zeros((B, H, dh, dh), jnp.float32), jnp.moveaxis(kv, 1, 0))
    states = jnp.moveaxis(states, 0, 1)
    o_cross = jnp.einsum('bncht,bnhte->bnche', qc * q_dec[:, :, None], states)
    o = (o_intra + o_cross).reshape(B, S, H, dh)
    mu = jnp.mean(o, axis=-1, keepdims=True)
    var = jnp.mean(jnp.square(o - mu), axis=-1, keepdims=True)
    o = ((o - mu) * lax.rsqrt(var + GN_EPS)).reshape(B, S, RET_WIDTH)
    return jax.nn.silu(g.astype(jnp.float32)) * o

def rglru(xr, gr, conv_w, conv_b, w_ra, b_ra, w_ri, b_ri, lam):
    B, S = xr.shape[:2]
    x = xr.astype(jnp.float32)
    pad = jnp.pad(x, ((0, 0), (CONV_WIDTH - 1, 0), (0, 0)))
    xc = conv_b + sum(conv_w[kk] * pad[:, kk:kk + S] for kk in range(CONV_WIDTH))
    xh = xc.reshape(B, S, LRU_BLOCKS, LRU_BLOCK_DIM)
    r = jax.nn.sigmoid(jnp.einsum('bsgi,gij->bsgj', xh, w_ra).reshape(B, S, LRU_WIDTH) + b_ra)
    i = jax.nn.sigmoid(jnp.einsum('bsgi,gij->bsgj', xh, w_ri).reshape(B, S, LRU_WIDTH) + b_ri)
    log_a = LRU_C * r * jax.nn.log_sigmoid(lam.astype(jnp.float32))
    a = jnp.exp(log_a)
    b = jnp.sqrt(-jnp.expm1(2.0 * log_a)) * (i * xc)

    def combine(e1, e2):
        a1, b1 = e1
        a2, b2 = e2
        return a1 * a2, a2 * b1 + b2

    _, h = lax.associative_scan(combine, (a, b), axis=1)
    return h * jax.nn.gelu(gr.astype(jnp.float32))

def peer(x, w_pq, sub_keys, peer_u, peer_v):
    B, S, D = x.shape
    xt = x.reshape(-1, PEER_TOKEN_BLOCK, D)
    K = PEER_TOPK

    def block(xb):
        q = (xb @ w_pq).reshape(PEER_TOKEN_BLOCK, PEER_HEADS, 2, PEER_HALF)
        s1 = jnp.einsum('thd,hnd->thn', q[:, :, 0], sub_keys[:, 0])
        s2 = jnp.einsum('thd,hnd->thn', q[:, :, 1], sub_keys[:, 1])
        v1, i1 = lax.top_k(s1, K)
        v2, i2 = lax.top_k(s2, K)
        cand = (v1[..., :, None] + v2[..., None, :]).reshape(PEER_TOKEN_BLOCK, PEER_HEADS, K * K)
        vs, ci = lax.top_k(cand, K)
        e1 = jnp.take_along_axis(i1, ci // K, axis=-1)
        e2 = jnp.take_along_axis(i2, ci % K, axis=-1)
        expert = e1 * N_KEYS + e2
        gates = jax.nn.softmax(vs.astype(jnp.float32), axis=-1)
        u = peer_u[expert]
        act = jax.nn.gelu(jnp.einsum('thkd,td->thk', u, xb))
        return jnp.einsum('thk,thkd->td', gates * act, peer_v[expert])

    return lax.map(block, xt).reshape(B, S, D)

def setup_inputs(seed: int = 0) -> dict:
    key = jax.random.key(seed)
    ks = jax.random.split(key, 18)
    f32 = jnp.float32
    x = jax.random.normal(ks[0], (BATCH, SEQ, D_MODEL), f32)
    positions = jnp.broadcast_to(jnp.arange(SEQ, dtype=jnp.int32), (BATCH, SEQ))
    col_scale = jnp.concatenate([
        jnp.ones((2 * RET_WIDTH,), f32), jnp.full((RET_WIDTH,), DN_BETA, f32),
        jnp.ones((RET_WIDTH,), f32), jnp.full((LRU_WIDTH,), DN_BETA, f32),
        jnp.ones((LRU_WIDTH,), f32)])
    w_in = jax.random.normal(ks[1], (DEPTH, D_MODEL, IN_COLS), f32) * (D_MODEL ** -0.5) * col_scale
    w_out = jax.random.normal(ks[2], (DEPTH, MIX_WIDTH, D_MODEL), f32) * (MIX_WIDTH ** -0.5) * DN_BETA
    conv_w = jax.random.normal(ks[3], (DEPTH, CONV_WIDTH, LRU_WIDTH), f32) * (CONV_WIDTH ** -0.5)
    conv_b = 0.01 * jax.random.normal(ks[4], (DEPTH, LRU_WIDTH), f32)
    w_ra = jax.random.normal(ks[5], (DEPTH, LRU_BLOCKS, LRU_BLOCK_DIM, LRU_BLOCK_DIM), f32) * (LRU_BLOCK_DIM ** -0.5)
    b_ra = 0.01 * jax.random.normal(ks[6], (DEPTH, LRU_WIDTH), f32)
    w_ri = jax.random.normal(ks[7], (DEPTH, LRU_BLOCKS, LRU_BLOCK_DIM, LRU_BLOCK_DIM), f32) * (LRU_BLOCK_DIM ** -0.5)
    b_ri = 0.01 * jax.random.normal(ks[8], (DEPTH, LRU_WIDTH), f32)
    a_c = jax.random.uniform(ks[9], (DEPTH, LRU_WIDTH), f32, minval=0.9, maxval=0.999)
    a0 = a_c ** (1.0 / LRU_C)
    lru_lambda = jnp.log(a0) - jnp.log1p(-a0)
    ln1_g = 1.0 + 0.02 * jax.random.normal(ks[10], (DEPTH, D_MODEL), f32)
    ln1_b = 0.02 * jax.random.normal(ks[11], (DEPTH, D_MODEL), f32)
    w_pq = jax.random.normal(ks[12], (DEPTH, D_MODEL, PEER_HEADS * PEER_QUERY_DIM), f32) * (D_MODEL ** -0.5)
    sub_keys = jax.random.normal(ks[13], (DEPTH, PEER_HEADS, 2, N_KEYS, PEER_HALF), f32) * (PEER_HALF ** -0.5)
    peer_u = jax.random.normal(ks[14], (DEPTH, N_EXPERTS, D_MODEL), f32) * (D_MODEL ** -0.5)
    peer_v = jax.random.normal(ks[15], (DEPTH, N_EXPERTS, D_MODEL), f32) * DN_BETA
    ln2_g = 1.0 + 0.02 * jax.random.normal(ks[16], (DEPTH, D_MODEL), f32)
    ln2_b = 0.02 * jax.random.normal(ks[17], (DEPTH, D_MODEL), f32)
    return {"x": x, "positions": positions, "w_in": w_in, "w_out": w_out,
            "conv_w": conv_w, "conv_b": conv_b, "w_ra": w_ra, "b_ra": b_ra,
            "w_ri": w_ri, "b_ri": b_ri, "lru_lambda": lru_lambda,
            "ln1_g": ln1_g, "ln1_b": ln1_b, "w_pq": w_pq, "sub_keys": sub_keys,
            "peer_u": peer_u, "peer_v": peer_v, "ln2_g": ln2_g, "ln2_b": ln2_b}

def reference(x, positions, w_in, w_out, conv_w, conv_b, w_ra, b_ra, w_ri, b_ri, lru_lambda,
              ln1_g, ln1_b, w_pq, sub_keys, peer_u, peer_v, ln2_g, ln2_b):
    R, L = RET_WIDTH, LRU_WIDTH
    h = x
    for l in range(DEPTH):
        proj = h @ w_in[l]
        q, k, v, g, xr, gr = jnp.split(proj, [R, 2 * R, 3 * R, 4 * R, 4 * R + L], axis=-1)
        y_ret = retention(q, k, v, g, positions)
        y_lru = rglru(xr, gr, conv_w[l], conv_b[l], w_ra[l], b_ra[l], w_ri[l], b_ri[l], lru_lambda[l])
        mix = jnp.concatenate([y_ret, y_lru], axis=-1) @ w_out[l]
        h = layer_norm(DN_ALPHA * h + mix, ln1_g[l], ln1_b[l])
        h = layer_norm(DN_ALPHA * h + peer(h, w_pq[l], sub_keys[l], peer_u[l], peer_v[l]), ln2_g[l], ln2_b[l])
    return h


_drawn_inputs = setup_inputs


def setup_inputs(seed=0):
    import zlib

    import numpy as np

    out = dict(_drawn_inputs(seed))
    spreads = {}
    factors = {'b_ra': 44.572, 'b_ri': 35.468, 'ln2_g': 8.439, 'ln2_b': 8.211}
    for name, (base, spread) in spreads.items():
        noise = np.random.default_rng([zlib.crc32(name.encode()), seed]).standard_normal(out[name].shape)
        drawn = base * np.exp(spread * noise) if base else spread * noise
        out[name] = __import__('jax').numpy.asarray(drawn.astype(out[name].dtype))
    for name, factor in factors.items():
        out[name] = (out[name] * factor).astype(out[name].dtype)
    return out
```

```python
from contextlib import ExitStack

import concourse.bass as bass
from concourse import mybir

F32 = mybir.dt.float32
I32 = mybir.dt.int32
U32 = mybir.dt.uint32
ALU = mybir.AluOpType
ACT = mybir.ActivationFunctionType
AX = mybir.AxisListType

P = 128
SEQ = 512
D = 2048
TT = SEQ // P
KT = D // P
HEADS = 8
CHUNK = 64
K = 16
NKEYS = 128
NW = 4
BANK = 512
COLS = 512
NG = 8
ALPHA = 2.0 ** 0.25
LN_EPS = 1e-5
GN_EPS = 1e-6
LRU_C = 8.0
NEG = -3.0e38
ROUND = 1.5 * 2.0 ** 23

U_VG, U_LRU, U_QK, U_OUT, U_PQ, U_END = 0, 16, 32, 48, 64, 80


def two_pi_parts():
    import math
    parts, rest = [], 2 * math.pi
    for n in range(4):
        step = 2.0 ** (-9 - 12 * n)
        part = float(int(rest / step)) * step if n < 3 else rest
        parts.append(part)
        rest -= part
    return parts


def build(nc, x_tok, x_t, positions, w_units, gate_w, chan, sub_t, ln1_t, ln_rows, peer_u, peer_v,
          ident_c, decay_c, freq_c, iota_c, out):
    ctx = ExitStack()
    with ctx:
        def sb(name, shape, dt=F32):
            return ctx.enter_context(nc.sbuf_tensor(name, shape, dt))

        def sem(name):
            return ctx.enter_context(nc.semaphore(name))

        big = sb("big", [P, KT * SEQ + 2 * NKEYS])
        vg = sb("vg", [P, TT, D])
        ring = sb("ring", [P, NG, D])
        h_tok = sb("h_tok", [P, TT, D])
        rows = sb("rows", [P, 2, D])
        work = sb("work", [P, 10 * BANK])
        mid = sb("mid", [P, 4 * BANK])
        ident = sb("ident", [P, P])
        iota = sb("iota", [P, K])
        chan_sb = sb("chan_sb", [P, 8, HEADS])
        c8 = sb("c8", [P, HEADS])
        small = sb("small", [P, 128])
        topk = sb("topk", [P, 200])
        gates = sb("gates", [P, 2, K])
        eidx = sb("eidx", [P, 2, K], U32)
        freq = sb("freq", [P, 1])
        ln1_col = sb("ln1_col", [P, 2, KT])

        xT = big[:, 0:KT * SEQ].rearrange("p (k t) -> p k t", k=KT)
        keys = big[:, :].rearrange("p (g n) -> p g n", n=2 * NKEYS)
        keys_by_unit = big[:, 0:KT * SEQ].rearrange("p (t m n) -> p t m n", t=TT, n=NKEYS)
        hT = vg[:, :, :].rearrange("p t d -> p (t d)").rearrange("p (k t) -> p k t", k=KT)
        mixT = ring[:, 0:4, :].rearrange("p s d -> p (s d)").rearrange("p (k t) -> p k t", k=KT)
        wslot = [ring[:, NG - NW + s, :] for s in range(NW)]
        decay = rows[:, :, :].rearrange("p a d -> p (a d)").rearrange("p (h t) -> p h t", h=HEADS)
        w = [work[:, n * BANK:(n + 1) * BANK] for n in range(10)]
        cosT, sinT = mid[:, 0:BANK], mid[:, BANK:2 * BANK]
        sub_sb = mid[:, :].rearrange("p (n k) -> p n k", k=NKEYS)
        wgate = mid[:, 2 * BANK:3 * BANK].rearrange("p (b a n) -> p b a n", b=2, a=2)
        xc = [w[0], w[1]]
        rgate, igate, a_t, th, gelu_gr, den, s_in, hscan = w[2], w[3], w[4], w[5], w[6], w[7], w[8], w[9]
        qT, kT, rot = [w[0], w[1]], [w[2], w[3]], [w[4], w[5]]
        probs = work[:, 6 * BANK:10 * BANK].rearrange("p (i t) -> p i t", i=TT)
        normed = mid[:, 2 * BANK:3 * BANK].rearrange("p (c e) -> p c e", c=TT)
        qpT = [w[0], w[1]]
        diag = work[:, 0:4 * BANK].rearrange("p (j t) -> p j t", j=K)
        y_out = work[:, 4 * BANK:8 * BANK]
        s_cp, s_low = work[:, 4096:4352], work[:, 4352:4480]
        cand, cand_low = work[:, 4480:4736], work[:, 4736:4992]
        pick = mid[:, 0:256].rearrange("p (k j) -> p k j", j=K)
        pick2 = mid[:, 256:512].rearrange("p (k j) -> p k j", j=K)
        alpha_id = mid[:, 512:640]
        act_u = mid[:, 640:656]
        act_g = mid[:, 656:672]
        wgt = mid[:, 672:688]
        v1, v2 = topk[:, 0:16], topk[:, 16:32]
        i1, i2, ci = topk[:, 32:48].bitcast(U32), topk[:, 48:64].bitcast(U32), topk[:, 64:80].bitcast(U32)
        i1f, i2f = topk[:, 80:96], topk[:, 96:112]
        vs = topk[:, 112:128]
        c1, c2 = topk[:, 128:144].bitcast(U32), topk[:, 144:160].bitcast(U32)
        cf, e1 = topk[:, 160:176], topk[:, 176:192]
        ssum, rsum = topk[:, 192:193], topk[:, 193:194]
        stats = small[:, 0:96].rearrange("p (t c s) -> p t c s", t=TT, c=4)
        mv = small[:, 96:104].rearrange("p (t s) -> p t s", t=TT)
        sd, rstd = small[:, 104:108], small[:, 108:112]
        lam = [small[:, 8 * n:8 * n + 8] for n in range(8)]
        ang, turns, hi_turns, prod = w[2], w[3], w[4], w[5]
        pos_i = work[:, 3072:3584].bitcast(I32)

        psum = ctx.enter_context(nc.psum_tensor("psum", [P, 8, BANK], F32))

        def bank(n):
            return psum[:, n, :]

        x_landed = [sem(f"x_landed{n}") for n in range(4)]
        w_landed = [sem(f"w_landed{n}") for n in range(NW)]
        consts_landed = sem("consts_landed")
        decay_landed = sem("decay_landed")
        tok_landed = sem("tok_landed")
        gate_landed = [sem("gate_landed0"), sem("gate_landed1")]
        rows_landed = sem("rows_landed")
        rows2_landed = sem("rows2_landed")
        sub_landed = sem("sub_landed")
        units_done = sem("units_done")
        vg_bank_done = sem("vg_bank_done")
        vg_bank_free = sem("vg_bank_free")
        lam_ready = sem("lam_ready")
        c8_ready = sem("c8_ready")
        trig_ready = sem("trig_ready")
        sin_done = sem("sin_done")
        conv_done = sem("conv_done")
        gates_mm = sem("gates_mm")
        lru_act = sem("lru_act")
        sq_ready = sem("sq_ready")
        sq_done = sem("sq_done")
        lru_done = sem("lru_done")
        rot_q = sem("rot_q")
        rot_k = sem("rot_k")
        scores_mm = sem("scores_mm")
        masked = sem("masked")
        o_mm = sem("o_mm")
        var_ready = sem("var_ready")
        sd_ready = sem("sd_ready")
        ret_done = sem("ret_done")
        ret_tr = sem("ret_tr")
        ret_copied = sem("ret_copied")
        mix_bank_done = sem("mix_bank_done")
        mix_added = sem("mix_added")
        ln1_normed = sem("ln1_normed")
        h_tr = sem("h_tr")
        h_copied = sem("h_copied")
        h_ready = sem("h_ready")
        qp_copied = sem("qp_copied")
        key_mm = sem("key_mm")
        keys_copied = sem("keys_copied")
        picked = sem("picked")
        exp_in = sem("exp_in")
        exp_out = sem("exp_out")
        g_landed = [sem(f"g_landed{n}") for n in range(NG)]
        slot_seen_free = sem("slot_seen_free")
        u_used = sem("u_used")
        v_used = sem("v_used")
        gelu_out = sem("gelu_out")
        diag_ready = sem("diag_ready")
        acc_read = sem("acc_read")
        y_ready = sem("y_ready")
        y_stored = sem("y_stored")
        y_free = sem("y_free")
        out_v = out.rearrange("b (t p) d -> (b t) p d", p=P)

        block = ctx.enter_context(nc.Block())

        @block.sync
        def _(sp):
            for s in range(NW):
                sp.dma_start(xT[:, 4 * s:4 * s + 4, :], x_t[s]).then_inc(x_landed[s], 16)
                sp.dma_start(wslot[s], w_units[s]).then_inc(w_landed[s], 16)
            with sp.Fori(1, U_END // NW) as r:
                for s in range(NW):
                    sp.wait_ge(units_done, NW * r + s + 1 - NW)
                    sp.dma_start(wslot[s], w_units[NW * r + s]).then_inc(w_landed[s], 16)
            sp.sem_inc(y_free, 1)
            with sp.Fori(0, TT) as t:
                sp.wait_ge(y_ready, t + 1)
                sp.dma_start(out_v[t], y_out).then_inc(y_stored, 16)
                sp.wait_ge(y_stored, 16 * (t + 1))
                sp.sem_inc(y_free, 1)

        @block.scalar
        def _(act):
            act.dma_start(chan_sb[:, :, :], chan).then_inc(consts_landed, 16)
            act.dma_start(freq[:, :], freq_c).then_inc(consts_landed, 16)
            act.dma_start(pos_i, positions.partition_broadcast(P)).then_inc(consts_landed, 16)
            act.dma_start(ident[:, :], ident_c).then_inc(consts_landed, 16)
            act.dma_start(iota[:, :], iota_c).then_inc(consts_landed, 16)
            act.dma_start(ln1_col[:, :, :], ln1_t).then_inc(consts_landed, 16)
            act.dma_start(decay, decay_c).then_inc(decay_landed, 16)
            act.dma_start(h_tok[:, :, :], x_tok).then_inc(tok_landed, 16)
            act.wait_ge(lam_ready, 1)
            act.activation(lam[2], lam[1], ACT.Exp, scale=-1.0).then_inc(lam_ready, 1)
            act.wait_ge(trig_ready, 1)
            act.activation(sinT, sinT, ACT.Sin).then_inc(sin_done, 1)
            act.activation(cosT, cosT, ACT.Sin).then_inc(sin_done, 1)
            act.sem_inc(vg_bank_free, TT)
            for g in range(4):
                for t in range(TT):
                    act.wait_ge(vg_bank_done, TT * g + t + 1)
                    act.activation(vg[:, t, g * COLS:(g + 1) * COLS], bank(t),
                                   ACT.Copy if g < 2 else ACT.Silu).then_inc(vg_bank_free, 1)

            def lru(g, p):
                act.wait_ge(gates_mm, g + 1)
                if not isinstance(g, int) or g >= 1:
                    act.wait_ge(lru_done, g)
                act.activation(rgate, bank(4 * p + 2), ACT.Sigmoid, bias=chan_sb[:, 5, bass.ds(g, 1)])
                act.activation(igate, bank(4 * p + 3), ACT.Sigmoid, bias=chan_sb[:, 6, bass.ds(g, 1)])
                act.drain()
                act.activation(a_t, rgate, ACT.Exp, scale=c8[:, bass.ds(g, 1)])
                act.activation(th, rgate, ACT.Tanh, scale=c8[:, bass.ds(g, 1)]).then_inc(lru_act, 1)
                act.wait_ge(units_done, U_LRU + 2 * g + 2)
                act.activation(gelu_gr, bank(4 * p + 1), ACT.Gelu_apprx_tanh).then_inc(lru_act, 1)
                act.wait_ge(sq_ready, g + 1)
                act.activation(s_in, s_in, ACT.Sqrt).then_inc(sq_done, 1)

            act.wait_ge(c8_ready, 1)
            lru(0, 0)
            lru(1, 1)
            with act.Fori(1, HEADS // 2) as r:
                for p in range(2):
                    lru(2 * r + p, p)
            with act.Fori(0, HEADS) as h:
                act.wait_ge(var_ready, h + 1)
                act.activation(sd, sd, ACT.Sqrt).then_inc(sd_ready, 1)
            act.wait_ge(var_ready, HEADS + 1)
            act.activation(sd, sd, ACT.Sqrt).then_inc(sd_ready, 1)
            act.wait_ge(masked, TT * HEADS)
            act.dma_start(rows[:, :, :], ln_rows[0:2].partition_broadcast(P)).then_inc(rows_landed, 16)
            act.wait_ge(ret_done, HEADS)
            act.dma_start(sub_sb, sub_t).then_inc(sub_landed, 16)
            for k in range(KT):
                act.wait_ge(h_tr, k + 1)
                act.activation(hT[:, k, :], bank(k % 8), ACT.Identity, bias=ln1_col[:, 1, k:k + 1],
                               scale=ln1_col[:, 0, k:k + 1]).then_inc(h_copied, 1)
            def peer_q(n, p):
                act.wait_ge(units_done, U_PQ + n + 1)
                if not isinstance(n, int) or n >= 2:
                    act.wait_ge(key_mm, n - 1)
                act.activation(qpT[p], bank(p), ACT.Copy).then_inc(qp_copied, 1)

            def peer_s(n, p):
                act.wait_ge(key_mm, n + 1)
                act.activation(keys_by_unit[:, :, bass.ds(n, 1), :].rearrange("p t a n -> p t (a n)"),
                               bank(2 + p).rearrange("p (t n) -> p t n", t=TT),
                               ACT.Copy).then_inc(keys_copied, 1)

            for n in range(4):
                peer_q(n, n % 2)
                if n:
                    peer_s(n - 1, (n - 1) % 2)
            with act.Fori(1, 4) as r:
                for m in range(4):
                    peer_q(4 * r + m, m % 2)
                    peer_s(4 * r + m - 1, (m - 1) % 2)
            peer_s(15, 1)
            act.wait_ge(h_ready, 1)
            act.dma_start(rows[:, :, :], ln_rows[2:4].partition_broadcast(P)).then_inc(rows2_landed, 16)

            def softmax(g):
                act.wait_ge(exp_in, g + 1)
                act.activation(e1, cf, ACT.Exp, accum_out=ssum).then_inc(exp_out, 1)

            softmax(0)
            with act.Fori(0, TT) as t:
                with act.Fori(0, HEADS) as h:
                    act.wait_ge(u_used, (t * HEADS + h) * K + K)
                    act.activation(act_g, act_u, ACT.Gelu_apprx_tanh).then_inc(gelu_out, 1)
                    softmax(t * HEADS + h + 1)
                act.wait_ge(var_ready, HEADS + 2 + t)
                act.activation(sd[:, 0:1], sd[:, 0:1], ACT.Sqrt).then_inc(sd_ready, 1)

        @block.gpsimd
        def _(pool):
            for p in range(2):
                pool.dma_start(wgate[:, p, :, :], gate_w[p]).then_inc(gate_landed[p], 16)
            with pool.Fori(1, HEADS // 2) as r:
                for p in range(2):
                    pool.wait_ge(gates_mm, 2 * r + p - 1)
                    pool.dma_start(wgate[:, p, :, :], gate_w[2 * r + p]).then_inc(gate_landed[p], 16)

            def gather(slot, table, par, j):
                pool.sem_inc(slot_seen_free, 1)
                pool.indirect_dma_start(ring[:, slot, :], None, table,
                                        bass.IndirectOffsetOnAxis(eidx[:, par, j:j + 1], 0)
                                        ).then_inc(g_landed[slot], 16)

            with pool.Fori(0, TT * HEADS // 2) as r:
                for par in range(2):
                    g = 2 * r + par
                    pool.wait_ge(picked, g + 1)
                    for j in range(K):
                        s = j % NG
                        if j < NG:
                            pool.wait_ge(v_used, K * g + j + NG + 1)
                        else:
                            pool.wait_ge(u_used, K * g + j - NG + 1)
                        gather(s, peer_u, par, j)
                    for j in range(K):
                        s = j % NG
                        if j < NG:
                            pool.wait_ge(u_used, K * g + j + NG + 1)
                        else:
                            pool.wait_ge(v_used, K * g + K + j - NG + 1)
                        gather(s, peer_v, par, j)

        @block.vector
        def _(dve):
            dve.wait_ge(consts_landed, 16 * 6)
            lam_in = chan_sb[:, 7, :]
            dve.scalar_tensor_tensor(out=lam[1], in0=lam_in, scalar=-1.0, in1=lam_in, op0=ALU.mult, op1=ALU.max).then_inc(lam_ready, 1)
            dve.wait_ge(lam_ready, 2)
            dve.tensor_scalar(lam[3], lam[2], 2.0, None, ALU.add)
            dve.drain()
            dve.reciprocal(lam[4], lam[3])
            dve.drain()
            dve.tensor_tensor(lam[3], lam[2], lam[4], ALU.mult)
            dve.drain()
            dve.tensor_tensor(lam[4], lam[3], lam[3], ALU.mult)
            dve.drain()
            dve.tensor_scalar(lam[5], lam[4], 1.0 / 19, None, ALU.mult)
            dve.drain()
            for n in range(8, 0, -1):
                a, b = (5, 6) if n % 2 == 0 else (6, 5)
                dve.scalar_tensor_tensor(out=lam[b], in0=lam[a], scalar=1.0 / (2 * n + 1), in1=lam[4],
                                         op0=ALU.add, op1=ALU.mult)
                dve.drain()
            dve.tensor_scalar(lam[6], lam[5], 1.0, 2.0, ALU.add, ALU.mult)
            dve.tensor_scalar(lam[2], lam_in, 0.0, None, ALU.min)
            dve.drain()
            dve.tensor_tensor(lam[7], lam[6], lam[3], ALU.mult)
            dve.drain()
            dve.tensor_tensor(lam[6], lam[2], lam[7], ALU.subtract)
            dve.drain()
            dve.tensor_scalar(c8[:, :], lam[6], LRU_C, None, ALU.mult).then_inc(c8_ready, 1)
            dve.tensor_copy(ang, pos_i)
            dve.drain()
            dve.tensor_scalar(ang, ang, freq[:, 0:1], None, ALU.mult)
            dve.drain()
            dve.tensor_scalar(turns, ang, 0.15915494309189535, ROUND, ALU.mult, ALU.add)
            dve.drain()
            dve.tensor_scalar(turns, turns, -ROUND, None, ALU.add)
            dve.drain()
            dve.tensor_scalar(hi_turns, turns, 2.0 ** -11, ROUND, ALU.mult, ALU.add)
            dve.drain()
            dve.tensor_scalar(hi_turns, hi_turns, -ROUND, 2.0 ** 11, ALU.add, ALU.mult)
            dve.drain()
            dve.tensor_tensor(turns, turns, hi_turns, ALU.subtract)
            dve.drain()
            for part in two_pi_parts():
                for n in (hi_turns, turns):
                    dve.scalar_tensor_tensor(out=ang, in0=n, scalar=-part, in1=ang, op0=ALU.mult,
                                             op1=ALU.add)
                    dve.drain()
            dve.tensor_scalar(ang, ang, 3.1415925, -3.1415925, ALU.min, ALU.max)
            dve.drain()
            dve.tensor_scalar(sinT[0:64], ang[0:64], 1.0, None, ALU.mult)
            dve.tensor_scalar(sinT[64:128], ang[64:128], -1.0, None, ALU.mult)
            dve.scalar_tensor_tensor(out=prod, in0=ang, scalar=-1.0, in1=ang, op0=ALU.mult, op1=ALU.max)
            dve.drain()
            dve.tensor_scalar(cosT, prod, -1.0, 1.5707963267948966, ALU.mult, ALU.add).then_inc(trig_ready, 1)
            dve.wait_ge(sin_done, 2)

            def conv(g, p):
                dve.wait_ge(units_done, U_LRU + 2 * g + 1)
                src = bank(4 * p)

                def tap(n):
                    return chan_sb[:, n, bass.ds(g, 1)]
                dve.tensor_scalar(xc[p], src, tap(3), tap(4), ALU.mult, ALU.add)
                for back in range(1, 4):
                    dve.drain()
                    last = dve.scalar_tensor_tensor(out=xc[p][:, back:SEQ], in0=src[:, 0:SEQ - back],
                                                    scalar=tap(3 - back), in1=xc[p][:, back:SEQ],
                                                    op0=ALU.mult, op1=ALU.add)
                last.then_inc(conv_done, 1)

            def lru(g, p):
                dve.wait_ge(lru_act, 2 * g + 1)
                dve.tensor_tensor(igate, igate, xc[p], ALU.mult)
                dve.tensor_scalar(den, th, -1.0, 1.0, ALU.mult, ALU.add)
                dve.drain()
                dve.reciprocal(hscan, den)
                dve.drain()
                dve.scalar_tensor_tensor(out=s_in, in0=th, scalar=-2.0, in1=hscan, op0=ALU.mult,
                                         op1=ALU.mult).then_inc(sq_ready, 1)
                dve.wait_ge(sq_done, g + 1)
                dve.tensor_tensor(den, s_in, igate, ALU.mult)
                dve.drain()
                dve.tensor_tensor_scan(out=hscan, data0=a_t, data1=den, initial=0.0, op0=ALU.mult,
                                       op1=ALU.add)
                dve.drain()
                dve.wait_ge(lru_act, 2 * g + 2)
                dve.tensor_tensor(mixT[:, bass.ds(HEADS + g, 1), :].rearrange("p a t -> p (a t)"),
                                  hscan, gelu_gr, ALU.mult).then_inc(lru_done, 1)
                dve.drain()

            conv(0, 0)
            conv(1, 1)
            lru(0, 0)
            with dve.Fori(1, HEADS // 2) as r:
                conv(2 * r, 0)
                lru(2 * r - 1, 1)
                conv(2 * r + 1, 1)
                lru(2 * r, 0)
            lru(HEADS - 1, 1)

            def rotate(src, dst, done):
                dve.tensor_tensor(rot[0], src, cosT, ALU.mult)
                dve.tensor_tensor(rot[1][0:64], src[64:128], sinT[64:128], ALU.mult)
                dve.tensor_tensor(rot[1][64:128], src[0:64], sinT[0:64], ALU.mult)
                dve.drain()
                dve.tensor_tensor(dst, rot[0], rot[1], ALU.add).then_inc(done, 1)
                dve.drain()

            def rotate_q(h, p):
                dve.wait_ge(units_done, U_QK + 2 * h + 1)
                rotate(bank(p), qT[p], rot_q)

            def rotate_k(h, p):
                dve.wait_ge(units_done, U_QK + 2 * h + 2)
                rotate(bank(2 + p), kT[p], rot_k)

            def mask(h):
                for i in range(TT):
                    n = SEQ - P * i
                    dve.wait_ge(scores_mm, TT * h + i + 1)
                    dve.tensor_tensor(probs[:, i, 0:n], bank(4 + i % 2)[:, 0:n],
                                      decay[:, bass.ds(h, 1), 0:n].rearrange("p a t -> p (a t)"),
                                      ALU.mult).then_inc(masked, 1)

            def group_norm(h, p):
                dve.wait_ge(o_mm, h + 1)
                o = bank(6 + p).rearrange("p (c e) -> p c e", c=TT)
                for c in range(TT):
                    dve.bn_stats(stats[:, c, 0, :], o[:, c, :])
                dve.drain()
                for c in range(TT):
                    dve.bn_aggr(mv[:, c, :], stats[:, c, 0, :])
                dve.drain()
                dve.tensor_scalar(sd, mv[:, :, 1], GN_EPS, None, ALU.add).then_inc(var_ready, 1)
                dve.wait_ge(sd_ready, h + 1)
                dve.reciprocal(rstd, sd)
                dve.drain()
                for c in range(TT):
                    dve.tensor_scalar(normed[:, c, :], o[:, c, :], mv[:, c, 0:1], rstd[:, c:c + 1],
                                      ALU.subtract, ALU.mult)
                dve.drain()
                gate = vg[:, :, bass.ds(1024 + P * h, P)]
                dve.tensor_tensor(gate, normed, gate, ALU.mult).then_inc(ret_done, 1)
                dve.drain()

            dve.wait_ge(decay_landed, 16)
            rotate_q(0, 0)
            rotate_k(0, 0)
            rotate_q(1, 1)
            mask(0)
            rotate_k(1, 1)
            group_norm(0, 0)
            with dve.Fori(1, HEADS // 2) as r:
                for p in range(2):
                    h = 2 * r + p
                    rotate_q(h, p)
                    mask(h - 1)
                    rotate_k(h, p)
                    group_norm(h - 1, 1 - p)
            mask(HEADS - 1)
            group_norm(HEADS - 1, 1)
            for h in range(HEADS):
                dve.wait_ge(ret_tr, h + 1)
                dve.tensor_copy(mixT[:, h, :], bank(4 + h % 3)).then_inc(ret_copied, 1)

            dve.wait_ge(tok_landed, 16)
            with dve.Fori(0, 4) as c:
                for t in range(TT):
                    dve.wait_ge(mix_bank_done, TT * c + t + 1)
                    cols = h_tok[:, t, bass.ds(c * COLS, COLS)]
                    dve.scalar_tensor_tensor(out=cols, in0=cols, scalar=ALPHA, in1=bank(t), op0=ALU.mult,
                                             op1=ALU.add).then_inc(mix_added, 1)
                    dve.drain()
                    dve.bn_stats(stats[:, t, bass.ds(c, 1), :].rearrange("p a s -> p (a s)"), cols)
            dve.drain()
            for t in range(TT):
                dve.bn_aggr(mv[:, t, :], stats[:, t, :, :])
            dve.drain()
            dve.tensor_scalar(sd, mv[:, :, 1], LN_EPS, None, ALU.add).then_inc(var_ready, 1)
            dve.wait_ge(sd_ready, HEADS + 1)
            dve.reciprocal(rstd, sd)
            dve.drain()
            for t in range(TT):
                dve.tensor_scalar(h_tok[:, t, :], h_tok[:, t, :], mv[:, t, 0:1], rstd[:, t:t + 1],
                                  ALU.subtract, ALU.mult).then_inc(ln1_normed, 1)
            dve.wait_ge(rows_landed, 16)
            dve.wait_ge(h_tr, KT)
            for t in range(TT):
                dve.drain()
                dve.tensor_tensor(h_tok[:, t, :], h_tok[:, t, :], rows[:, 0, :], ALU.mult)
                dve.drain()
                last = dve.tensor_tensor(h_tok[:, t, :], h_tok[:, t, :], rows[:, 1, :], ALU.add)
            last.then_inc(h_ready, 1)

            def top16(vals, idx, src, low):
                dve.max(vals[:, 0:8], src)
                dve.drain()
                dve.max_index(idx[:, 0:8], vals[:, 0:8], src)
                dve.match_replace(low, vals[:, 0:8], src, NEG)
                dve.drain()
                dve.max(vals[:, 8:16], low)
                dve.drain()
                dve.max_index(idx[:, 8:16], vals[:, 8:16], low)
                dve.drain()

            def over_j(ap):
                return ap.rearrange("p (k a) -> p k a", a=1).broadcast_to([P, K, K])

            def over_k(ap):
                return ap.rearrange("p (a j) -> p a j", a=1).broadcast_to([P, K, K])

            def choose(g, par):
                dve.drain()
                dve.tensor_copy(s_cp, keys[:, bass.ds(g, 1), :].rearrange("p a n -> p (a n)"))
                dve.drain()
                top16(v1, i1, s_cp[:, 0:NKEYS], s_low)
                top16(v2, i2, s_cp[:, NKEYS:2 * NKEYS], s_low)
                dve.tensor_tensor(cand.rearrange("p (k j) -> p k j", j=K), over_j(v1), over_k(v2), ALU.add)
                dve.tensor_copy(i1f, i1)
                dve.tensor_copy(i2f, i2)
                dve.drain()
                top16(vs, ci, cand, cand_low)
                dve.tensor_scalar(c1, ci, 4, None, ALU.logical_shift_right)
                dve.tensor_scalar(c2, ci, 15, None, ALU.bitwise_and)
                dve.drain()
                dve.tensor_copy(cf, c1)
                dve.drain()
                dve.tensor_tensor(pick, over_j(cf), over_k(iota[:, :]), ALU.is_equal)
                dve.drain()
                dve.tensor_tensor(pick2, pick, over_k(i1f), ALU.mult)
                dve.drain()
                dve.tensor_reduce(e1, pick2, AX.X, ALU.add)
                dve.tensor_copy(cf, c2)
                dve.drain()
                dve.tensor_tensor(pick, over_j(cf), over_k(iota[:, :]), ALU.is_equal)
                dve.drain()
                dve.tensor_tensor(pick2, pick, over_k(i2f), ALU.mult)
                dve.drain()
                dve.tensor_reduce(cf, pick2, AX.X, ALU.add)
                dve.drain()
                dve.scalar_tensor_tensor(out=eidx[:, par, :], in0=e1, scalar=float(NKEYS), in1=cf,
                                         op0=ALU.mult, op1=ALU.add).then_inc(picked, 1)
                dve.drain()
                dve.tensor_scalar(cf, vs, vs[:, 0:1], None, ALU.subtract).then_inc(exp_in, 1)
                dve.wait_ge(exp_out, g + 1)
                dve.reciprocal(rsum, ssum)
                dve.drain()
                dve.tensor_scalar(gates[:, par, :], e1, rsum, None, ALU.mult)
                dve.drain()

            dve.wait_ge(keys_copied, 2 * HEADS)
            dve.tensor_scalar(alpha_id, ident[:, :], ALPHA, None, ALU.mult)
            dve.memset(keys[:, TT * HEADS, :], 0.0)
            dve.drain().then_inc(acc_read, 1)
            choose(0, 0)
            dve.wait_ge(rows2_landed, 16)
            with dve.Fori(0, TT) as t:
                with dve.Fori(0, HEADS // 2) as hp:
                    for par in range(2):
                        g = t * HEADS + 2 * hp + par
                        row = h_tok[:, bass.ds(t, 1), :].rearrange("p a d -> p (a d)")
                        for j in range(K):
                            s = j % NG
                            dve.wait_ge(g_landed[s], 16 * (4 * g + j // NG + 1))
                            dve.scalar_tensor_tensor(out=ring[:, s, :], in0=ring[:, s, :], scalar=1.0,
                                                     in1=row, op0=ALU.mult, op1=ALU.mult,
                                                     accum_out=act_u[:, j:j + 1]).then_inc(u_used, 1)
                        dve.wait_ge(gelu_out, g + 1)
                        dve.tensor_tensor(wgt, act_g, gates[:, par, :], ALU.mult)
                        dve.drain()
                        dve.wait_ge(v_used, K * g + K)
                        dve.tensor_tensor(diag, ident[:, :].rearrange("p (a t) -> p a t", a=1).broadcast_to([P, K, P]),
                                          wgt.rearrange("p (j a) -> p j a", a=1).broadcast_to([P, K, P]),
                                          ALU.mult).then_inc(diag_ready, 1)
                        choose(g + 1, 1 - par)
                dve.wait_ge(v_used, K * HEADS * (t + 1) + K)
                for c in range(4):
                    dve.bn_stats(stats[:, 0, c, :], bank(c))
                dve.drain()
                dve.bn_aggr(mv[:, 0, :], stats[:, 0, :, :])
                dve.drain()
                dve.tensor_scalar(sd[:, 0:1], mv[:, 0, 1:2], LN_EPS, None, ALU.add).then_inc(var_ready, 1)
                dve.wait_ge(sd_ready, HEADS + 2 + t)
                dve.reciprocal(rstd[:, 0:1], sd[:, 0:1])
                dve.drain()
                dve.wait_ge(y_free, t + 1)
                dve.tensor_scalar(y_out, psum[:, 0:4, :].rearrange("p a n -> p (a n)"), mv[:, 0, 0:1],
                                  rstd[:, 0:1], ALU.subtract, ALU.mult).then_inc(acc_read, 1)
                dve.drain()
                dve.tensor_tensor(y_out, y_out, rows[:, 0, :], ALU.mult)
                dve.drain()
                dve.tensor_tensor(y_out, y_out, rows[:, 1, :], ALU.add).then_inc(y_ready, 1)

        @block.tensor
        def _(pe):
            def stationary_unit(dst, slot, source, wait=None):
                wt = wslot[slot].rearrange("p (k n) -> p k n", n=P)
                for k in range(KT):
                    if wait is not None:
                        pe.wait_ge(wait, k + 1)
                    mm = pe.matmul(dst, wt[:, k, :], source[:, k, :], start=(k == 0), stop=(k == KT - 1))
                mm.then_inc(units_done, 1)

            def moving_group(c, source, order, first_unit, done, freed, extra=None):
                for q in range(4):
                    pe.wait_ge(w_landed[q], 16 * (first_unit // NW + c + 1))
                    wt = wslot[q].rearrange("p (k n) -> p k n", n=COLS)
                    if extra is not None:
                        extra(q)
                    for t in range(TT):
                        if q == 0 and freed is not None:
                            pe.wait_ge(*freed(t))
                        for k in range(4):
                            mm = pe.matmul(bank(t), source[:, order[4 * q + k], P * t:P * t + P], wt[:, k, :],
                                           start=(q == 0 and k == 0), stop=(q == 3 and k == 3))
                        if q == 3:
                            mm.then_inc(done, 1)
                    if q < 3:
                        mm.then_inc(units_done, 1)
                    else:
                        pe.drain().then_inc(units_done, 1)

            for n in range(4):
                pe.wait_ge(x_landed[n], 16)
            with pe.Fori(0, 4) as c:
                moving_group(c, xT, list(range(KT)), U_VG, vg_bank_done,
                             lambda t: (vg_bank_free, TT * c + t + 1))

            def lru_gates(g, p):
                pe.wait_ge(gate_landed[p], 8 * (g - p) + 16)
                pe.wait_ge(conv_done, g + 1)
                pe.matmul(bank(4 * p + 2), wgate[:, p, 0, :], xc[p], start=True, stop=True)
                pe.matmul(bank(4 * p + 3), wgate[:, p, 1, :], xc[p], start=True, stop=True).then_inc(gates_mm, 1)

            def lru_block(g, p, first):
                pe.wait_ge(w_landed[2 * p], 16 * (U_LRU // 4) + 8 * (g - p) + 16)
                if not first:
                    pe.wait_ge(lru_done, g - 1)
                stationary_unit(bank(4 * p), 2 * p, xT)

            def lru_block_gr(g, p):
                pe.wait_ge(w_landed[2 * p + 1], 16 * (U_LRU // 4) + 8 * (g - p) + 16)
                stationary_unit(bank(4 * p + 1), 2 * p + 1, xT)

            pe.wait_ge(vg_bank_free, 5 * TT)
            lru_block(0, 0, True)
            lru_block_gr(0, 0)
            lru_block(1, 1, True)
            lru_gates(0, 0)
            lru_block_gr(1, 1)
            with pe.Fori(1, HEADS // 2) as r:
                for p in range(2):
                    g = 2 * r + p
                    lru_block(g, p, False)
                    lru_gates(g - 1, 1 - p)
                    lru_block_gr(g, p)
            lru_gates(HEADS - 1, 1)

            def head_q(h, p, first):
                pe.wait_ge(w_landed[2 * p], 16 * (U_QK // 4) + 8 * (h - p) + 16)
                if not first:
                    pe.wait_ge(rot_q, h - 1)
                stationary_unit(bank(p), 2 * p, xT)

            def head_k(h, p, first):
                pe.wait_ge(w_landed[2 * p + 1], 16 * (U_QK // 4) + 8 * (h - p) + 16)
                if not first:
                    pe.wait_ge(rot_k, h - 1)
                stationary_unit(bank(2 + p), 2 * p + 1, xT)

            def scores(h, p, first=False):
                pe.wait_ge(rot_q, h + 1)
                pe.wait_ge(rot_k, h + 1)
                for i in range(TT):
                    if not (first and i < 2):
                        pe.wait_ge(masked, TT * h + i - 1)
                    pe.matmul(bank(4 + i % 2)[:, 0:SEQ - P * i], kT[p][:, P * i:P * i + P],
                              qT[p][:, P * i:SEQ], start=True, stop=True).then_inc(scores_mm, 1)

            def outputs(h, p):
                pe.wait_ge(masked, TT * (h + 1))
                for c in range(TT):
                    for i in range(c + 1):
                        mm = pe.matmul(bank(6 + p)[:, P * c:P * c + P], probs[:, i, P * (c - i):P * (c - i + 1)],
                                       vg[:, i, bass.ds(P * h, P)], start=(i == 0), stop=(i == c))
                mm.then_inc(o_mm, 1)

            pe.wait_ge(lru_done, HEADS)
            head_q(0, 0, True)
            head_k(0, 0, True)
            head_q(1, 1, True)
            scores(0, 0, True)
            head_k(1, 1, True)
            outputs(0, 0)
            with pe.Fori(1, HEADS // 2) as r:
                for p in range(2):
                    h = 2 * r + p
                    head_q(h, p, False)
                    scores(h - 1, 1 - p)
                    head_k(h, p, False)
                    outputs(h - 1, 1 - p)
            scores(HEADS - 1, 1)
            outputs(HEADS - 1, 1)

            def turn_retention(q):
                if q != 2:
                    return
                for h in range(HEADS):
                    pe.wait_ge(ret_done, h + 1)
                    if h >= 3:
                        pe.wait_ge(ret_copied, h - 2)
                    for t in range(TT):
                        mm = pe.transpose(bank(4 + h % 3)[:, P * t:P * t + P],
                                          vg[:, t, 1024 + P * h:1024 + P * h + P], ident[:, :])
                    mm.then_inc(ret_tr, 1)
                pe.wait_ge(ret_copied, HEADS)

            mix_order = list(range(HEADS, KT)) + list(range(HEADS))
            moving_group(0, mixT, mix_order, U_OUT, mix_bank_done, None, turn_retention)
            with pe.Fori(1, 4) as c:
                moving_group(c, mixT, mix_order, U_OUT, mix_bank_done,
                             lambda t: (mix_added, TT * (c - 1) + t + 1))

            pe.wait_ge(ln1_normed, TT)
            for k in range(KT):
                if k >= 8:
                    pe.wait_ge(h_copied, k - 7)
                for t in range(TT):
                    mm = pe.transpose(bank(k % 8)[:, P * t:P * t + P], h_tok[:, t, P * k:P * k + P],
                                      ident[:, :])
                mm.then_inc(h_tr, 1)
            pe.wait_ge(h_copied, KT)

            def queries(n, p, slot, r, first):
                pe.wait_ge(w_landed[slot], 16 * (U_PQ // 4 + r + 1))
                if not first:
                    pe.wait_ge(qp_copied, n - 1)
                stationary_unit(bank(p), slot, hT)

            def key_scores(n, p, first):
                pe.wait_ge(qp_copied, n + 1)
                if not first:
                    pe.wait_ge(keys_copied, n - 1)
                for t in range(TT):
                    mm = pe.matmul(bank(2 + p)[:, P * t:P * t + P], qpT[p][:, P * t:P * t + P],
                                   sub_sb[:, bass.ds(n, 1), :].rearrange("p a k -> p (a k)"),
                                   start=True, stop=True)
                mm.then_inc(key_mm, 1)

            pe.wait_ge(sub_landed, 16)
            for n in range(4):
                queries(n, n % 2, n, 0, n < 2)
                if n:
                    key_scores(n - 1, (n - 1) % 2, n < 3)
            with pe.Fori(1, 4) as r:
                for m in range(4):
                    n = 4 * r + m
                    queries(n, m % 2, m, r, False)
                    key_scores(n - 1, (m - 1) % 2, False)
            key_scores(15, 1, False)

            pe.sem_inc(v_used, K)
            with pe.Fori(0, TT) as t:
                pe.wait_ge(acc_read, t + 1)
                for c in range(4):
                    pe.matmul(bank(c), alpha_id, h_tok[:, bass.ds(t, 1), c * BANK:(c + 1) * BANK
                                                       ].rearrange("p a d -> p (a d)"),
                              start=True, stop=False, skip_group_check=True)
                with pe.Fori(0, HEADS) as h:
                    g = t * HEADS + h
                    pe.wait_ge(diag_ready, g + 1)
                    for j in range(K):
                        s = j % NG
                        pe.wait_ge(g_landed[s], 16 * (4 * g + 2 + j // NG + 1))
                        for c in range(4):
                            mm = pe.matmul(bank(c), diag[:, j, :], ring[:, s, c * BANK:(c + 1) * BANK],
                                           start=False, stop=True, skip_group_check=True)
                        mm.then_inc(v_used, 1)


_OUT_SHAPE = (1, SEQ, D)


def _constants():
    import numpy as np
    half = P // 2
    freq = (10000.0 ** (-(np.arange(half, dtype=np.float32)) / np.float32(half))).astype(np.float32)
    m = np.arange(P)[:, None]
    c = np.arange(SEQ)[None, :]
    same, later = c // CHUNK == m // CHUNK, c // CHUNK > m // CHUNK
    gap = np.where(same, np.abs(c - m), c - m).astype(np.float64)
    decay = np.zeros((P, HEADS, SEQ), np.float32)
    for h in range(HEADS):
        gamma = 1.0 - 2.0 ** (-5.0 - h)
        decay[:, h, :] = np.where(same | later, gamma ** np.maximum(gap, 0.0), 0.0) * P ** -0.5
    return {
        "ident_c": np.eye(P, dtype=np.float32),
        "decay_c": decay,
        "freq_c": np.concatenate([freq, freq])[:, None],
        "iota_c": np.tile(np.arange(K, dtype=np.float32), (P, 1)),
    }


def _stationary(wt, columns):
    return wt[:, columns].reshape(KT, P, -1, P).transpose(2, 1, 0, 3).reshape(-1, P, KT * P)


def _moving(wt, order):
    t = wt.reshape(KT, P, -1, COLS)[order]
    return t.reshape(4, 4, P, -1, COLS).transpose(3, 0, 2, 1, 4).reshape(-1, P, 4 * COLS)


def kernel(x, positions, w_in, w_out, conv_w, conv_b, w_ra, b_ra, w_ri, b_ri, lru_lambda,
           ln1_g, ln1_b, w_pq, sub_keys, peer_u, peer_v, ln2_g, ln2_b):
    import numpy as np
    import concourse.bacc as bacc
    from concourse.bass_utils import run_bass_kernel_spmd

    x, w_in, w_out, w_pq = np.asarray(x)[0], np.asarray(w_in)[0], np.asarray(w_out)[0], np.asarray(w_pq)[0]

    def turns(a, b):
        return np.concatenate([np.r_[s + P * n:s + P * n + P] for n in range(HEADS) for s in (a, b)])

    natural = list(range(KT))
    units = np.concatenate([
        _moving(w_in[:, 2048:4096], natural),
        _stationary(w_in, turns(4096, 5120)),
        _stationary(w_in, turns(0, 1024)),
        _moving(w_out, natural[HEADS:] + natural[:HEADS]),
        _stationary(w_pq, slice(None)),
    ])
    per_channel = [np.asarray(conv_w)[0][n] for n in range(4)] + [
        np.asarray(a)[0] for a in (conv_b, b_ra, b_ri, lru_lambda)]
    arrays = {
        "x_tok": np.ascontiguousarray(x.reshape(TT, P, D).transpose(1, 0, 2)),
        "x_t": np.ascontiguousarray(x.T.reshape(4, 4, P, SEQ).transpose(0, 2, 1, 3)),
        "positions": np.ascontiguousarray(positions),
        "w_units": np.ascontiguousarray(units),
        "gate_w": np.ascontiguousarray(np.stack([np.asarray(w_ra)[0], np.asarray(w_ri)[0]], 1)
                                       .transpose(0, 2, 1, 3)),
        "chan": np.ascontiguousarray(np.stack(per_channel).reshape(8, HEADS, P).transpose(2, 0, 1)),
        "sub_t": np.ascontiguousarray(np.asarray(sub_keys)[0].reshape(KT, NKEYS, P).transpose(2, 0, 1)),
        "ln1_t": np.ascontiguousarray(np.stack([np.asarray(ln1_g)[0], np.asarray(ln1_b)[0]])
                                      .reshape(2, KT, P).transpose(2, 0, 1)),
        "ln_rows": np.ascontiguousarray(np.concatenate([np.asarray(a) for a in (ln1_g, ln1_b, ln2_g, ln2_b)])),
        "peer_u": np.ascontiguousarray(np.asarray(peer_u)[0]),
        "peer_v": np.ascontiguousarray(np.asarray(peer_v)[0]),
        **_constants(),
    }
    nc = bacc.Bacc("TRN2", target_bir_lowering=False, num_devices=1)
    aps = {n: nc.dram_tensor(n, a.shape, mybir.dt.from_np(a.dtype), kind="ExternalInput").ap()
           for n, a in arrays.items()}
    out = nc.dram_tensor("out", _OUT_SHAPE, F32, kind="ExternalOutput").ap()
    build(nc, out=out, **aps)
    result = run_bass_kernel_spmd(nc, [arrays], core_ids=[0])
    return result.results[0]["out"]
```

```python
from contextlib import ExitStack

import concourse.bass as bass
from concourse import mybir

F32 = mybir.dt.float32
I32 = mybir.dt.int32
U32 = mybir.dt.uint32
ALU = mybir.AluOpType
ACT = mybir.ActivationFunctionType
AX = mybir.AxisListType

P = 128
SEQ = 512
D = 2048
TT = SEQ // P
KT = D // P
HEADS = 8
CHUNK = 64
K = 16
NKEYS = 128
NW = 4
BANK = 512
COLS = 512
NG = 8
NG1 = 4
EXPERTS = NKEYS * NKEYS
CHUNKS = EXPERTS // COLS
DENSE = TT - 1
ALPHA = 2.0 ** 0.25
LN_EPS = 1e-5
GN_EPS = 1e-6
LRU_C = 8.0
NEG = -3.0e38
ROUND = 1.5 * 2.0 ** 23

U_VG, U_LRU, U_QK, U_OUT, U_PQ, U_PEER = 0, 16, 32, 48, 64, 80
U_END = U_PEER + NW * CHUNKS


def two_pi_parts():
    import math
    parts, rest = [], 2 * math.pi
    for n in range(4):
        step = 2.0 ** (-9 - 12 * n)
        part = float(int(rest / step)) * step if n < 3 else rest
        parts.append(part)
        rest -= part
    return parts


def build(nc, x_tok, x_t, positions, w_units, u_units, gate_w, chan, sub_t, ln1_t, ln_rows, peer_u, peer_v,
          ident_c, decay_c, freq_c, iota_c, base_c, out):
    ctx = ExitStack()
    with ctx:
        def sb(name, shape, dt=F32):
            return ctx.enter_context(nc.sbuf_tensor(name, shape, dt))

        def sem(name):
            return ctx.enter_context(nc.semaphore(name))

        big = sb("big", [P, KT * SEQ + 2 * NKEYS])
        vg = sb("vg", [P, TT, D])
        ring = sb("ring", [P, NG, D])
        h_tok = sb("h_tok", [P, TT, D])
        rows = sb("rows", [P, 2, D])
        work = sb("work", [P, 10 * BANK])
        mid = sb("mid", [P, 4 * BANK])
        ident = sb("ident", [P, P])
        iota = sb("iota", [P, K])
        chan_sb = sb("chan_sb", [P, 8, HEADS])
        c8 = sb("c8", [P, HEADS])
        small = sb("small", [P, 128])
        topk = sb("topk", [P, 260])
        freq = sb("freq", [P, 1])
        base = sb("base", [P, TT * HEADS + 1])
        ln1_col = sb("ln1_col", [P, 2, KT])

        xT = big[:, 0:KT * SEQ].rearrange("p (k t) -> p k t", k=KT)
        keys = big[:, :].rearrange("p (g n) -> p g n", n=2 * NKEYS)
        keys_by_unit = big[:, 0:KT * SEQ].rearrange("p (t m n) -> p t m n", t=TT, n=NKEYS)
        hT = vg[:, :, :].rearrange("p t d -> p (t d)").rearrange("p (k t) -> p k t", k=KT)
        mixT = ring[:, 0:4, :].rearrange("p s d -> p (s d)").rearrange("p (k t) -> p k t", k=KT)
        wslot = [ring[:, NG - NW + s, :] for s in range(NW)]
        decay = rows[:, :, :].rearrange("p a d -> p (a d)").rearrange("p (h t) -> p h t", h=HEADS)
        w = [work[:, n * BANK:(n + 1) * BANK] for n in range(10)]
        cosT, sinT = mid[:, 0:BANK], mid[:, BANK:2 * BANK]
        sub_sb = mid[:, :].rearrange("p (n k) -> p n k", k=NKEYS)
        wgate = mid[:, 2 * BANK:3 * BANK].rearrange("p (b a n) -> p b a n", b=2, a=2)
        xc = [w[0], w[1]]
        rgate, igate, a_t, th, gelu_gr, den, s_in, hscan = w[2], w[3], w[4], w[5], w[6], w[7], w[8], w[9]
        qT, kT, rot = [w[0], w[1]], [w[2], w[3]], [w[4], w[5]]
        probs = work[:, 6 * BANK:10 * BANK].rearrange("p (i t) -> p i t", i=TT)
        normed = mid[:, 2 * BANK:3 * BANK].rearrange("p (c e) -> p c e", c=TT)
        qpT = [w[0], w[1]]
        score_st = work[:, 0:3072].rearrange("p (b t e) -> p b t e", b=2, t=DENSE)
        s_cp, s_low = work[:, 3072:3328], mid[:, 1296:1552]
        cand, cand_low = work[:, 3456:3712], work[:, 3712:3968]
        eidx = work[:, 3968:4496].bitcast(U32)
        vidx = work[:, 4496:5024].bitcast(U32)
        gates = mid[:, 768:1296]
        acc0 = rows[:, 0, :]
        rows2 = vg[:, 0:2, :]
        pick1 = mid[:, 0:256].rearrange("p (k j) -> p k j", j=K)
        pick2 = mid[:, 256:512].rearrange("p (k j) -> p k j", j=K)
        act_u = mid[:, 512:544].rearrange("p (b j) -> p b j", b=2)
        act_g = mid[:, 544:560]
        wgt = mid[:, 560:576]
        eidx_st = mid[:, 576:608].bitcast(U32).rearrange("p (b j) -> p b j", b=2)
        vidx_st = mid[:, 608:640].bitcast(U32).rearrange("p (b j) -> p b j", b=2)
        v1, v2 = topk[:, 0:16], topk[:, 16:32]
        i1, i2, ci = topk[:, 32:48].bitcast(U32), topk[:, 48:64].bitcast(U32), topk[:, 64:80].bitcast(U32)
        i1f, i2f = topk[:, 80:96], topk[:, 96:112]
        vs = topk[:, 112:128]
        c1, c2 = topk[:, 128:144].bitcast(U32), topk[:, 144:160].bitcast(U32)
        c1f, c2f, e1, e2 = (topk[:, 160 + 16 * n:176 + 16 * n] for n in range(4))
        less, expo = topk[:, 224:240], topk[:, 240:256]
        ssum, rsum = topk[:, 256:257], topk[:, 257:258]
        stats = small[:, 0:96].rearrange("p (t c s) -> p t c s", t=TT, c=4)
        mv = small[:, 96:104].rearrange("p (t s) -> p t s", t=TT)
        sd, rstd = small[:, 104:108], small[:, 108:112]
        lam = [small[:, 8 * n:8 * n + 8] for n in range(8)]
        ang, turns, hi_turns, prod = w[2], w[3], w[4], w[5]
        pos_i = work[:, 3072:3584].bitcast(I32)

        psum = ctx.enter_context(nc.psum_tensor("psum", [P, 8, BANK], F32))

        def bank(n):
            return psum[:, n, :]

        x_landed = [sem(f"x_landed{n}") for n in range(4)]
        w_landed = [sem(f"w_landed{n}") for n in range(NW)]
        consts_landed = sem("consts_landed")
        decay_landed = sem("decay_landed")
        tok_landed = sem("tok_landed")
        gate_landed = [sem("gate_landed0"), sem("gate_landed1")]
        rows_landed = sem("rows_landed")
        rows2_landed = sem("rows2_landed")
        sub_landed = sem("sub_landed")
        units_done = sem("units_done")
        vg_bank_done = sem("vg_bank_done")
        vg_bank_free = sem("vg_bank_free")
        lam_ready = sem("lam_ready")
        c8_ready = sem("c8_ready")
        trig_ready = sem("trig_ready")
        sin_done = sem("sin_done")
        conv_done = sem("conv_done")
        gates_mm = sem("gates_mm")
        lru_act = sem("lru_act")
        sq_ready = sem("sq_ready")
        sq_done = sem("sq_done")
        lru_done = sem("lru_done")
        rot_q = sem("rot_q")
        rot_k = sem("rot_k")
        scores_mm = sem("scores_mm")
        masked = sem("masked")
        o_mm = sem("o_mm")
        var_ready = sem("var_ready")
        sd_ready = sem("sd_ready")
        ret_done = sem("ret_done")
        ret_tr = sem("ret_tr")
        ret_copied = sem("ret_copied")
        mix_bank_done = sem("mix_bank_done")
        mix_added = sem("mix_added")
        ln1_normed = sem("ln1_normed")
        h_tr = sem("h_tr")
        h_copied = sem("h_copied")
        qp_copied = sem("qp_copied")
        key_mm = sem("key_mm")
        keys_copied = sem("keys_copied")
        exp_in = sem("exp_in")
        exp_out = sem("exp_out")
        g_landed = [sem(f"g_landed{n}") for n in range(NG)]
        slot_seen_free = sem("slot_seen_free")
        u_used = sem("u_used")
        v_used = sem("v_used")
        gelu_out = sem("gelu_out")
        score_bank_done = sem("score_bank_done")
        score_copied = sem("score_copied")
        score_stored = [sem("score_stored0"), sem("score_stored1")]
        staged = sem("staged")
        staged_v = sem("staged_v")
        val_landed = [sem("val_landed0"), sem("val_landed1")]
        wgt_ready = sem("wgt_ready")
        y_ready = sem("y_ready")
        y_stored = sem("y_stored")
        products = nc.dram_tensor("products", (DENSE * P * EXPERTS, 1), F32, kind="Internal").ap()
        products_v = products.rearrange("(t p e) a -> p t (e a)", t=DENSE, e=EXPERTS)
        out_v = out.rearrange("b (t p) d -> (b t) p d", p=P)

        block = ctx.enter_context(nc.Block())

        @block.sync
        def _(sp):
            for s in range(NW):
                sp.dma_start(xT[:, 4 * s:4 * s + 4, :], x_t[s]).then_inc(x_landed[s], 16)
                sp.dma_start(wslot[s], w_units[s]).then_inc(w_landed[s], 16)
            with sp.Fori(1, U_PEER // NW) as r:
                for s in range(NW):
                    sp.wait_ge(units_done, NW * r + s + 1 - NW)
                    sp.dma_start(wslot[s], w_units[NW * r + s]).then_inc(w_landed[s], 16)
            with sp.Fori(0, CHUNKS) as c:
                for s in range(NW):
                    sp.wait_ge(units_done, U_PEER + NW * c + s + 1 - NW)
                    sp.dma_start(wslot[s], u_units[NW * c + s]).then_inc(w_landed[s], 16)
            sp.wait_ge(y_ready, 1)
            sp.dma_start(out_v[0], acc0).then_inc(y_stored, 16)
            with sp.Fori(1, TT) as t:
                sp.wait_ge(y_ready, t + 1)
                sp.dma_start(out_v[t], h_tok[:, bass.ds(t, 1), :].rearrange("p a d -> p (a d)")
                             ).then_inc(y_stored, 16)
            sp.wait_ge(y_stored, 16 * TT)

        @block.scalar
        def _(act):
            act.dma_start(chan_sb[:, :, :], chan).then_inc(consts_landed, 16)
            act.dma_start(freq[:, :], freq_c).then_inc(consts_landed, 16)
            act.dma_start(pos_i, positions.partition_broadcast(P)).then_inc(consts_landed, 16)
            act.dma_start(ident[:, :], ident_c).then_inc(consts_landed, 16)
            act.dma_start(iota[:, :], iota_c).then_inc(consts_landed, 16)
            act.dma_start(ln1_col[:, :, :], ln1_t).then_inc(consts_landed, 16)
            act.dma_start(base[:, :], base_c).then_inc(consts_landed, 16)
            act.wait_ge(lam_ready, 1)
            act.activation(lam[2], lam[1], ACT.Exp, scale=-1.0).then_inc(lam_ready, 1)
            act.wait_ge(trig_ready, 1)
            act.activation(sinT, sinT, ACT.Sin).then_inc(sin_done, 1)
            act.activation(cosT, cosT, ACT.Sin).then_inc(sin_done, 1)
            for g in range(4):
                if g == 1:
                    act.dma_start(decay, decay_c).then_inc(decay_landed, 16)
                    act.dma_start(h_tok[:, :, :], x_tok).then_inc(tok_landed, 16)
                for t in range(TT):
                    act.wait_ge(vg_bank_done, TT * g + t + 1)
                    act.activation(vg[:, t, g * COLS:(g + 1) * COLS], bank(t),
                                   ACT.Copy if g < 2 else ACT.Silu).then_inc(vg_bank_free, 1)

            def lru(g, p):
                act.wait_ge(gates_mm, g + 1)
                if not isinstance(g, int) or g >= 1:
                    act.wait_ge(lru_done, g)
                act.activation(rgate, bank(4 * p + 2), ACT.Sigmoid, bias=chan_sb[:, 5, bass.ds(g, 1)])
                act.activation(igate, bank(4 * p + 3), ACT.Sigmoid, bias=chan_sb[:, 6, bass.ds(g, 1)])
                act.drain()
                act.activation(a_t, rgate, ACT.Exp, scale=c8[:, bass.ds(g, 1)])
                act.activation(th, rgate, ACT.Tanh, scale=c8[:, bass.ds(g, 1)]).then_inc(lru_act, 1)
                act.wait_ge(units_done, U_LRU + 2 * g + 2)
                act.activation(gelu_gr, bank(4 * p + 1), ACT.Gelu_apprx_tanh).then_inc(lru_act, 1)
                act.wait_ge(sq_ready, g + 1)
                act.activation(s_in, s_in, ACT.Sqrt).then_inc(sq_done, 1)

            act.wait_ge(c8_ready, 1)
            lru(0, 0)
            lru(1, 1)
            with act.Fori(1, HEADS // 2) as r:
                for p in range(2):
                    lru(2 * r + p, p)
            with act.Fori(0, HEADS) as h:
                act.wait_ge(var_ready, h + 1)
                act.activation(sd, sd, ACT.Sqrt).then_inc(sd_ready, 1)
            act.wait_ge(var_ready, HEADS + 1)
            act.activation(sd, sd, ACT.Sqrt).then_inc(sd_ready, 1)
            act.wait_ge(masked, TT * HEADS)
            act.dma_start(rows[:, :, :], ln_rows[0:2].partition_broadcast(P)).then_inc(rows_landed, 16)
            act.wait_ge(ret_done, HEADS)
            act.dma_start(sub_sb, sub_t).then_inc(sub_landed, 16)
            for k in range(KT):
                act.wait_ge(h_tr, k + 1)
                act.activation(hT[:, k, :], bank(k % 8), ACT.Identity, bias=ln1_col[:, 1, k:k + 1],
                               scale=ln1_col[:, 0, k:k + 1]).then_inc(h_copied, 1)
            def peer_q(n, p):
                act.wait_ge(units_done, U_PQ + n + 1)
                if not isinstance(n, int) or n >= 2:
                    act.wait_ge(key_mm, n - 1)
                act.activation(qpT[p], bank(p), ACT.Copy).then_inc(qp_copied, 1)

            def peer_s(n, p):
                act.wait_ge(key_mm, n + 1)
                act.activation(keys_by_unit[:, :, bass.ds(n, 1), :].rearrange("p t a n -> p t (a n)"),
                               bank(2 + p).rearrange("p (t n) -> p t n", t=TT),
                               ACT.Copy).then_inc(keys_copied, 1)

            for n in range(4):
                peer_q(n, n % 2)
                if n:
                    peer_s(n - 1, (n - 1) % 2)
            with act.Fori(1, 4) as r:
                for m in range(4):
                    peer_q(4 * r + m, m % 2)
                    peer_s(4 * r + m - 1, (m - 1) % 2)
            peer_s(15, 1)

            def softmax(g):
                act.wait_ge(exp_in, g + 1)
                act.activation(expo, less, ACT.Exp, accum_out=ssum).then_inc(exp_out, 1)

            def chunk(c, b, first):
                if not first:
                    act.wait_ge(score_stored[b], 8 * (c - b))
                for t in range(DENSE):
                    act.wait_ge(score_bank_done, DENSE * c + t + 1)
                    act.activation(score_st[:, b, t, :], bank(DENSE * b + t), ACT.Copy).then_inc(score_copied, 1)
                act.wait_ge(score_copied, DENSE * (c + 1) + 2 * DENSE)
                act.dma_start(products_v[:, :, bass.ds(c * COLS, COLS)], score_st[:, b, :, :]
                              ).then_inc(score_stored[b], 16)

            def sparse_group(h, first):
                softmax(4 * h + 1)
                chunk(4 * h, 0, first)
                act.wait_ge(u_used, h * K + K)
                act.activation(act_g, act_u[:, 0, :], ACT.Gelu_apprx_tanh).then_inc(gelu_out, 1)
                softmax(4 * h + 2)
                chunk(4 * h + 1, 1, first)
                softmax(4 * h + 3)
                chunk(4 * h + 2, 0, False)
                softmax(4 * h + 4)
                chunk(4 * h + 3, 1, False)

            act.sem_inc(score_copied, 2 * DENSE)
            softmax(0)
            sparse_group(0, True)
            with act.Fori(1, HEADS) as h:
                sparse_group(h, False)
            act.wait_ge(units_done, U_END)
            act.dma_start(rows2, ln_rows[2:4].partition_broadcast(P)).then_inc(rows2_landed, 16)

            def ln2_sd(t):
                act.wait_ge(var_ready, HEADS + 2 + t)
                act.activation(sd[:, 0:1], sd[:, 0:1], ACT.Sqrt).then_inc(sd_ready, 1)

            ln2_sd(0)
            with act.Fori(1, TT) as t:
                with act.Fori(0, HEADS // 2) as hp:
                    for par in range(2):
                        g = HEADS * t + 2 * hp + par
                        act.wait_ge(val_landed[par], 16 * K * (4 * (t - 1) + hp + 1))
                        act.wait_ge(wgt_ready, g)
                        act.activation(act_g, act_u[:, par, :], ACT.Gelu_apprx_tanh).then_inc(gelu_out, 1)
                ln2_sd(t)

        @block.gpsimd
        def _(pool):
            for p in range(2):
                pool.dma_start(wgate[:, p, :, :], gate_w[p]).then_inc(gate_landed[p], 16)
            with pool.Fori(1, HEADS // 2) as r:
                for p in range(2):
                    pool.wait_ge(gates_mm, 2 * r + p - 1)
                    pool.dma_start(wgate[:, p, :, :], gate_w[2 * r + p]).then_inc(gate_landed[p], 16)

            def gather(dst, table, idx, landed):
                pool.sem_inc(slot_seen_free, 1)
                pool.indirect_dma_start(dst, None, table, bass.IndirectOffsetOnAxis(idx, 0)
                                        ).then_inc(landed, 16)

            def first_tile_v(g):
                for j in range(K):
                    s = j % NG1
                    if j < NG1:
                        pool.wait_ge(u_used, K * g + K - NG1 + j + 1)
                    else:
                        pool.wait_ge(v_used, K * g + j - NG1 + 1)
                    gather(ring[:, s, :], peer_v, eidx_st[:, 1, j:j + 1], g_landed[s])

            def first_tile_u(g, first):
                for j in range(K):
                    s = j % NG1
                    if j >= NG1:
                        pool.wait_ge(u_used, K * g + j - NG1 + 1)
                    elif not first:
                        pool.wait_ge(v_used, K * g - NG1 + j + 1)
                    gather(ring[:, s, :], peer_u, eidx_st[:, 0, j:j + 1], g_landed[s])

            pool.wait_ge(staged, 1)
            first_tile_u(0, True)
            with pool.Fori(1, HEADS) as g:
                pool.wait_ge(staged_v, g)
                first_tile_v(g - 1)
                pool.wait_ge(staged, g + 1)
                first_tile_u(g, False)
            pool.wait_ge(staged_v, HEADS)
            first_tile_v(HEADS - 1)
            for b in range(2):
                pool.wait_ge(score_stored[b], 16 * CHUNKS // 2)
            pool.wait_ge(units_done, U_END)
            with pool.Fori(HEADS // 2, TT * HEADS // 2) as r:
                for par in range(2):
                    g = 2 * r + par
                    pool.wait_ge(staged, g + 2)
                    for j in range(K):
                        gather(act_u[:, par, j:j + 1], products, vidx_st[:, par, j:j + 1], val_landed[par])
                    for j in range(K):
                        s = j % NG
                        pool.wait_ge(v_used, K * g + j - NG + 1)
                        gather(ring[:, s, :], peer_v, eidx_st[:, par, j:j + 1], g_landed[s])

        @block.vector
        def _(dve):
            dve.wait_ge(consts_landed, 16 * 7)
            lam_in = chan_sb[:, 7, :]
            dve.scalar_tensor_tensor(out=lam[1], in0=lam_in, scalar=-1.0, in1=lam_in, op0=ALU.mult, op1=ALU.max).then_inc(lam_ready, 1)
            dve.wait_ge(lam_ready, 2)
            dve.tensor_scalar(lam[3], lam[2], 2.0, None, ALU.add)
            dve.drain()
            dve.reciprocal(lam[4], lam[3])
            dve.drain()
            dve.tensor_tensor(lam[3], lam[2], lam[4], ALU.mult)
            dve.drain()
            dve.tensor_tensor(lam[4], lam[3], lam[3], ALU.mult)
            dve.drain()
            dve.tensor_scalar(lam[5], lam[4], 1.0 / 19, None, ALU.mult)
            dve.drain()
            for n in range(8, 0, -1):
                a, b = (5, 6) if n % 2 == 0 else (6, 5)
                dve.scalar_tensor_tensor(out=lam[b], in0=lam[a], scalar=1.0 / (2 * n + 1), in1=lam[4],
                                         op0=ALU.add, op1=ALU.mult)
                dve.drain()
            dve.tensor_scalar(lam[6], lam[5], 1.0, 2.0, ALU.add, ALU.mult)
            dve.tensor_scalar(lam[2], lam_in, 0.0, None, ALU.min)
            dve.drain()
            dve.tensor_tensor(lam[7], lam[6], lam[3], ALU.mult)
            dve.drain()
            dve.tensor_tensor(lam[6], lam[2], lam[7], ALU.subtract)
            dve.drain()
            dve.tensor_scalar(c8[:, :], lam[6], LRU_C, None, ALU.mult).then_inc(c8_ready, 1)
            dve.tensor_copy(ang, pos_i)
            dve.drain()
            dve.tensor_scalar(ang, ang, freq[:, 0:1], None, ALU.mult)
            dve.drain()
            dve.tensor_scalar(turns, ang, 0.15915494309189535, ROUND, ALU.mult, ALU.add)
            dve.drain()
            dve.tensor_scalar(turns, turns, -ROUND, None, ALU.add)
            dve.drain()
            dve.tensor_scalar(hi_turns, turns, 2.0 ** -11, ROUND, ALU.mult, ALU.add)
            dve.drain()
            dve.tensor_scalar(hi_turns, hi_turns, -ROUND, 2.0 ** 11, ALU.add, ALU.mult)
            dve.drain()
            dve.tensor_tensor(turns, turns, hi_turns, ALU.subtract)
            dve.drain()
            for part in two_pi_parts():
                for n in (hi_turns, turns):
                    dve.scalar_tensor_tensor(out=ang, in0=n, scalar=-part, in1=ang, op0=ALU.mult,
                                             op1=ALU.add)
                    dve.drain()
            dve.tensor_scalar(ang, ang, 3.1415925, -3.1415925, ALU.min, ALU.max)
            dve.drain()
            dve.tensor_scalar(sinT[0:64], ang[0:64], 1.0, None, ALU.mult)
            dve.tensor_scalar(sinT[64:128], ang[64:128], -1.0, None, ALU.mult)
            dve.scalar_tensor_tensor(out=prod, in0=ang, scalar=-1.0, in1=ang, op0=ALU.mult, op1=ALU.max)
            dve.drain()
            dve.tensor_scalar(cosT, prod, -1.0, 1.5707963267948966, ALU.mult, ALU.add).then_inc(trig_ready, 1)
            dve.wait_ge(sin_done, 2)

            def conv(g, p):
                dve.wait_ge(units_done, U_LRU + 2 * g + 1)
                src = bank(4 * p)

                def tap(n):
                    return chan_sb[:, n, bass.ds(g, 1)]
                dve.tensor_scalar(xc[p], src, tap(3), tap(4), ALU.mult, ALU.add)
                for back in range(1, 4):
                    dve.drain()
                    last = dve.scalar_tensor_tensor(out=xc[p][:, back:SEQ], in0=src[:, 0:SEQ - back],
                                                    scalar=tap(3 - back), in1=xc[p][:, back:SEQ],
                                                    op0=ALU.mult, op1=ALU.add)
                last.then_inc(conv_done, 1)

            def lru(g, p):
                dve.wait_ge(lru_act, 2 * g + 1)
                dve.tensor_tensor(igate, igate, xc[p], ALU.mult)
                dve.tensor_scalar(den, th, -1.0, 1.0, ALU.mult, ALU.add)
                dve.drain()
                dve.reciprocal(hscan, den)
                dve.drain()
                dve.scalar_tensor_tensor(out=s_in, in0=th, scalar=-2.0, in1=hscan, op0=ALU.mult,
                                         op1=ALU.mult).then_inc(sq_ready, 1)
                dve.wait_ge(sq_done, g + 1)
                dve.tensor_tensor(den, s_in, igate, ALU.mult)
                dve.drain()
                dve.tensor_tensor_scan(out=hscan, data0=a_t, data1=den, initial=0.0, op0=ALU.mult,
                                       op1=ALU.add)
                dve.drain()
                dve.wait_ge(lru_act, 2 * g + 2)
                dve.tensor_tensor(mixT[:, bass.ds(HEADS + g, 1), :].rearrange("p a t -> p (a t)"),
                                  hscan, gelu_gr, ALU.mult).then_inc(lru_done, 1)
                dve.drain()

            conv(0, 0)
            conv(1, 1)
            lru(0, 0)
            with dve.Fori(1, HEADS // 2) as r:
                conv(2 * r, 0)
                lru(2 * r - 1, 1)
                conv(2 * r + 1, 1)
                lru(2 * r, 0)
            lru(HEADS - 1, 1)

            def rotate(src, dst, done):
                dve.tensor_tensor(rot[0], src, cosT, ALU.mult)
                dve.tensor_tensor(rot[1][0:64], src[64:128], sinT[64:128], ALU.mult)
                dve.tensor_tensor(rot[1][64:128], src[0:64], sinT[0:64], ALU.mult)
                dve.drain()
                dve.tensor_tensor(dst, rot[0], rot[1], ALU.add).then_inc(done, 1)
                dve.drain()

            def rotate_q(h, p):
                dve.wait_ge(units_done, U_QK + 2 * h + 1)
                rotate(bank(p), qT[p], rot_q)

            def rotate_k(h, p):
                dve.wait_ge(units_done, U_QK + 2 * h + 2)
                rotate(bank(2 + p), kT[p], rot_k)

            def mask(h):
                for i in range(TT):
                    n = SEQ - P * i
                    dve.wait_ge(scores_mm, TT * h + i + 1)
                    dve.tensor_tensor(probs[:, i, 0:n], bank(4 + i % 2)[:, 0:n],
                                      decay[:, bass.ds(h, 1), 0:n].rearrange("p a t -> p (a t)"),
                                      ALU.mult).then_inc(masked, 1)

            def group_norm(h, p):
                dve.wait_ge(o_mm, h + 1)
                o = bank(6 + p).rearrange("p (c e) -> p c e", c=TT)
                for c in range(TT):
                    dve.bn_stats(stats[:, c, 0, :], o[:, c, :])
                dve.drain()
                for c in range(TT):
                    dve.bn_aggr(mv[:, c, :], stats[:, c, 0, :])
                dve.drain()
                dve.tensor_scalar(sd, mv[:, :, 1], GN_EPS, None, ALU.add).then_inc(var_ready, 1)
                dve.wait_ge(sd_ready, h + 1)
                dve.reciprocal(rstd, sd)
                dve.drain()
                for c in range(TT):
                    dve.tensor_scalar(normed[:, c, :], o[:, c, :], mv[:, c, 0:1], rstd[:, c:c + 1],
                                      ALU.subtract, ALU.mult)
                dve.drain()
                gate = vg[:, :, bass.ds(1024 + P * h, P)]
                dve.tensor_tensor(gate, normed, gate, ALU.mult).then_inc(ret_done, 1)
                dve.drain()

            dve.wait_ge(decay_landed, 16)
            rotate_q(0, 0)
            rotate_k(0, 0)
            rotate_q(1, 1)
            mask(0)
            rotate_k(1, 1)
            group_norm(0, 0)
            with dve.Fori(1, HEADS // 2) as r:
                for p in range(2):
                    h = 2 * r + p
                    rotate_q(h, p)
                    mask(h - 1)
                    rotate_k(h, p)
                    group_norm(h - 1, 1 - p)
            mask(HEADS - 1)
            group_norm(HEADS - 1, 1)
            for h in range(HEADS):
                dve.wait_ge(ret_tr, h + 1)
                dve.tensor_copy(mixT[:, h, :], bank(4 + h % 3)).then_inc(ret_copied, 1)

            dve.wait_ge(tok_landed, 16)
            with dve.Fori(0, 4) as c:
                for t in range(TT):
                    dve.wait_ge(mix_bank_done, TT * c + t + 1)
                    cols = h_tok[:, t, bass.ds(c * COLS, COLS)]
                    dve.scalar_tensor_tensor(out=cols, in0=cols, scalar=ALPHA, in1=bank(t), op0=ALU.mult,
                                             op1=ALU.add).then_inc(mix_added, 1)
                    dve.drain()
                    dve.bn_stats(stats[:, t, bass.ds(c, 1), :].rearrange("p a s -> p (a s)"), cols)
            dve.drain()
            for t in range(TT):
                dve.bn_aggr(mv[:, t, :], stats[:, t, :, :])
            dve.drain()
            dve.tensor_scalar(sd, mv[:, :, 1], LN_EPS, None, ALU.add).then_inc(var_ready, 1)
            dve.wait_ge(sd_ready, HEADS + 1)
            dve.reciprocal(rstd, sd)
            dve.drain()
            for t in range(TT):
                dve.tensor_scalar(h_tok[:, t, :], h_tok[:, t, :], mv[:, t, 0:1], rstd[:, t:t + 1],
                                  ALU.subtract, ALU.mult).then_inc(ln1_normed, 1)
            dve.wait_ge(rows_landed, 16)
            dve.wait_ge(h_tr, KT)
            for t in range(TT):
                dve.drain()
                dve.tensor_tensor(h_tok[:, t, :], h_tok[:, t, :], rows[:, 0, :], ALU.mult)
                dve.drain()
                dve.tensor_tensor(h_tok[:, t, :], h_tok[:, t, :], rows[:, 1, :], ALU.add)
            dve.drain()

            def top16(*jobs):
                for vals, idx, src, low in jobs:
                    dve.max(vals[:, 0:8], src)
                dve.drain()
                for vals, idx, src, low in jobs:
                    dve.max_index(idx[:, 0:8], vals[:, 0:8], src)
                    dve.match_replace(low, vals[:, 0:8], src, NEG)
                dve.drain()
                for vals, idx, src, low in jobs:
                    dve.max(vals[:, 8:16], low)
                dve.drain()
                for vals, idx, src, low in jobs:
                    dve.max_index(idx[:, 8:16], vals[:, 8:16], low)
                dve.drain()

            def over_j(ap):
                return ap.rearrange("p (k a) -> p k a", a=1).broadcast_to([P, K, K])

            def over_k(ap):
                return ap.rearrange("p (a j) -> p a j", a=1).broadcast_to([P, K, K])

            def choose(g):
                dve.tensor_copy(s_cp, keys[:, bass.ds(g, 1), :].rearrange("p a n -> p (a n)"))
                dve.drain()
                top16((v1, i1, s_cp[:, 0:NKEYS], s_low[:, 0:NKEYS]),
                      (v2, i2, s_cp[:, NKEYS:2 * NKEYS], s_low[:, NKEYS:2 * NKEYS]))
                dve.tensor_tensor(cand.rearrange("p (k j) -> p k j", j=K), over_j(v1), over_k(v2), ALU.add)
                dve.tensor_copy(i1f, i1)
                dve.tensor_copy(i2f, i2)
                dve.drain()
                top16((vs, ci, cand, cand_low))
                dve.tensor_scalar(c1, ci, 4, None, ALU.logical_shift_right)
                dve.tensor_scalar(c2, ci, 15, None, ALU.bitwise_and)
                dve.drain()
                dve.tensor_copy(c1f, c1)
                dve.tensor_copy(c2f, c2)
                dve.drain()
                dve.tensor_tensor(pick1, over_j(c1f), over_k(iota[:, :]), ALU.is_equal)
                dve.tensor_tensor(pick2, over_j(c2f), over_k(iota[:, :]), ALU.is_equal)
                dve.drain()
                dve.tensor_tensor(pick1, pick1, over_k(i1f), ALU.mult)
                dve.tensor_tensor(pick2, pick2, over_k(i2f), ALU.mult)
                dve.drain()
                dve.tensor_reduce(e1, pick1, AX.X, ALU.add)
                dve.tensor_reduce(e2, pick2, AX.X, ALU.add)
                dve.tensor_scalar(less, vs, vs[:, 0:1], None, ALU.subtract).then_inc(exp_in, 1)
                dve.drain()
                span = bass.ds(g * K, K)
                dve.scalar_tensor_tensor(out=e1, in0=e1, scalar=float(NKEYS), in1=e2, op0=ALU.mult,
                                         op1=ALU.add)
                dve.drain()
                dve.tensor_copy(eidx[:, span], e1)
                dve.tensor_scalar(vidx[:, span], e1, base[:, bass.ds(g, 1)], None, ALU.add)
                dve.drain()
                dve.wait_ge(exp_out, g + 1)
                dve.reciprocal(rsum, ssum)
                dve.drain()
                dve.tensor_scalar(gates[:, span], expo, rsum, None, ALU.mult)
                dve.drain()

            dve.wait_ge(keys_copied, 2 * HEADS)
            dve.memset(keys[:, TT * HEADS, :], 0.0)
            dve.drain()
            choose(0)
            dve.tensor_scalar(acc0, h_tok[:, 0, :], ALPHA, None, ALU.mult)
            dve.drain()

            def stage(g, par):
                dve.tensor_copy(vidx_st[:, par, :], vidx[:, bass.ds(g * K, K)])
                dve.tensor_copy(eidx_st[:, par, :], eidx[:, bass.ds(g * K, K)])
                dve.drain().then_inc(staged, 1)

            def weigh(g):
                dve.wait_ge(gelu_out, g + 1)
                dve.tensor_tensor(wgt, act_g, gates[:, bass.ds(g * K, K)], ALU.mult).then_inc(wgt_ready, 1)
                dve.wait_ge(wgt_ready, g + 1)

            def add_rows(g, acc, slots, landed, js=range(K)):
                for j in js:
                    s = j % slots
                    dve.wait_ge(g_landed[s], landed(s, j // slots))
                    if j:
                        dve.wait_ge(v_used, K * g + j)
                    dve.scalar_tensor_tensor(out=acc, in0=ring[:, s, :], scalar=wgt[:, j:j + 1], in1=acc,
                                             op0=ALU.mult, op1=ALU.add).then_inc(v_used, 1)
                dve.wait_ge(v_used, K * g + js[-1] + 1)

            def second_ln(t, acc):
                for c in range(4):
                    dve.bn_stats(stats[:, 0, c, :], acc[:, c * BANK:(c + 1) * BANK])
                dve.drain()
                dve.bn_aggr(mv[:, 0, :], stats[:, 0, :, :])
                dve.drain()
                dve.tensor_scalar(sd[:, 0:1], mv[:, 0, 1:2], LN_EPS, None, ALU.add).then_inc(var_ready, 1)
                dve.wait_ge(sd_ready, HEADS + 2 + t)
                dve.reciprocal(rstd[:, 0:1], sd[:, 0:1])
                dve.drain()
                dve.tensor_scalar(acc, acc, mv[:, 0, 0:1], rstd[:, 0:1], ALU.subtract, ALU.mult)
                dve.drain()
                dve.tensor_tensor(acc, acc, rows2[:, 0, :], ALU.mult)
                dve.drain()
                dve.tensor_tensor(acc, acc, rows2[:, 1, :], ALU.add).then_inc(y_ready, 1)

            def stage_first(g, side, signal):
                dve.tensor_copy(eidx_st[:, side, :], eidx[:, bass.ds(g * K, K)]).then_inc(signal, 1)

            def products_u(g, js):
                for j in js:
                    s = j % NG1
                    dve.wait_ge(g_landed[s], 16 * (8 * g + j // NG1 + 1))
                    dve.scalar_tensor_tensor(out=ring[:, s, :], in0=ring[:, s, :], scalar=1.0,
                                             in1=h_tok[:, 0, :], op0=ALU.mult, op1=ALU.mult,
                                             accum_out=act_u[:, 0, j:j + 1]).then_inc(u_used, 1)

            def landed_first(g):
                return lambda s, n: 16 * (8 * g + 4 + n + 1)

            stage_first(0, 0, staged)
            with dve.Fori(0, HEADS) as g:
                stage_first(g, 1, staged_v)
                products_u(g, range(K // 2))
                choose(4 * g + 1)
                products_u(g, range(K // 2, K))
                stage_first(g + 1, 0, staged)
                choose(4 * g + 2)
                weigh(g)
                add_rows(g, acc0, NG1, landed_first(g), range(K // 2))
                choose(4 * g + 3)
                add_rows(g, acc0, NG1, landed_first(g), range(K // 2, K))
                choose(4 * g + 4)
            stage(HEADS, 0)
            dve.wait_ge(rows2_landed, 16)
            second_ln(0, acc0)
            with dve.Fori(1, TT) as t:
                acc = h_tok[:, bass.ds(t, 1), :].rearrange("p a d -> p (a d)")
                dve.tensor_scalar(acc, acc, ALPHA, None, ALU.mult)
                dve.drain()
                with dve.Fori(0, HEADS // 2) as hp:
                    for par in range(2):
                        g = t * HEADS + 2 * hp + par
                        stage(g + 1, 1 - par)
                        weigh(g)
                        add_rows(g, acc, NG, lambda s, n: (16 * 8 * HEADS if s < NG1 else 0)
                                 + 16 * (2 * (g - HEADS) + n + 1))
                second_ln(t, acc)

        @block.tensor
        def _(pe):
            def stationary_unit(dst, slot, source, wait=None):
                wt = wslot[slot].rearrange("p (k n) -> p k n", n=P)
                for k in range(KT):
                    if wait is not None:
                        pe.wait_ge(wait, k + 1)
                    mm = pe.matmul(dst, wt[:, k, :], source[:, k, :], start=(k == 0), stop=(k == KT - 1))
                mm.then_inc(units_done, 1)

            def moving_group(c, source, order, first_unit, done, freed, extra=None):
                for q in range(4):
                    pe.wait_ge(w_landed[q], 16 * (first_unit // NW + c + 1))
                    wt = wslot[q].rearrange("p (k n) -> p k n", n=COLS)
                    if extra is not None:
                        extra(q)
                    for t in range(TT):
                        if q == 0 and freed is not None:
                            pe.wait_ge(*freed(t))
                        for k in range(4):
                            mm = pe.matmul(bank(t), source[:, order[4 * q + k], P * t:P * t + P], wt[:, k, :],
                                           start=(q == 0 and k == 0), stop=(q == 3 and k == 3))
                        if q == 3:
                            mm.then_inc(done, 1)
                    if q < 3:
                        mm.then_inc(units_done, 1)
                    else:
                        pe.drain().then_inc(units_done, 1)

            natural = list(range(KT))
            moving_group(0, xT, natural, U_VG, vg_bank_done, None,
                         lambda q: pe.wait_ge(x_landed[q], 16))
            with pe.Fori(1, 4) as c:
                moving_group(c, xT, natural, U_VG, vg_bank_done,
                             lambda t: (vg_bank_free, TT * (c - 1) + t + 1))

            def lru_gates(g, p):
                pe.wait_ge(gate_landed[p], 8 * (g - p) + 16)
                pe.wait_ge(conv_done, g + 1)
                pe.matmul(bank(4 * p + 2), wgate[:, p, 0, :], xc[p], start=True, stop=True)
                pe.matmul(bank(4 * p + 3), wgate[:, p, 1, :], xc[p], start=True, stop=True).then_inc(gates_mm, 1)

            def lru_block(g, p, first):
                pe.wait_ge(w_landed[2 * p], 16 * (U_LRU // 4) + 8 * (g - p) + 16)
                if not first:
                    pe.wait_ge(lru_done, g - 1)
                stationary_unit(bank(4 * p), 2 * p, xT)

            def lru_block_gr(g, p):
                pe.wait_ge(w_landed[2 * p + 1], 16 * (U_LRU // 4) + 8 * (g - p) + 16)
                stationary_unit(bank(4 * p + 1), 2 * p + 1, xT)

            pe.wait_ge(vg_bank_free, 4 * TT)
            lru_block(0, 0, True)
            lru_block_gr(0, 0)
            lru_block(1, 1, True)
            lru_gates(0, 0)
            lru_block_gr(1, 1)
            with pe.Fori(1, HEADS // 2) as r:
                for p in range(2):
                    g = 2 * r + p
                    lru_block(g, p, False)
                    lru_gates(g - 1, 1 - p)
                    lru_block_gr(g, p)
            lru_gates(HEADS - 1, 1)

            def head_q(h, p, first):
                pe.wait_ge(w_landed[2 * p], 16 * (U_QK // 4) + 8 * (h - p) + 16)
                if not first:
                    pe.wait_ge(rot_q, h - 1)
                stationary_unit(bank(p), 2 * p, xT)

            def head_k(h, p, first):
                pe.wait_ge(w_landed[2 * p + 1], 16 * (U_QK // 4) + 8 * (h - p) + 16)
                if not first:
                    pe.wait_ge(rot_k, h - 1)
                stationary_unit(bank(2 + p), 2 * p + 1, xT)

            def scores(h, p, first=False):
                pe.wait_ge(rot_q, h + 1)
                pe.wait_ge(rot_k, h + 1)
                for i in range(TT):
                    if not (first and i < 2):
                        pe.wait_ge(masked, TT * h + i - 1)
                    pe.matmul(bank(4 + i % 2)[:, 0:SEQ - P * i], kT[p][:, P * i:P * i + P],
                              qT[p][:, P * i:SEQ], start=True, stop=True).then_inc(scores_mm, 1)

            def outputs(h, p):
                pe.wait_ge(masked, TT * (h + 1))
                for c in range(TT):
                    for i in range(c + 1):
                        mm = pe.matmul(bank(6 + p)[:, P * c:P * c + P], probs[:, i, P * (c - i):P * (c - i + 1)],
                                       vg[:, i, bass.ds(P * h, P)], start=(i == 0), stop=(i == c))
                mm.then_inc(o_mm, 1)

            pe.wait_ge(lru_done, HEADS)
            head_q(0, 0, True)
            head_k(0, 0, True)
            head_q(1, 1, True)
            scores(0, 0, True)
            head_k(1, 1, True)
            outputs(0, 0)
            with pe.Fori(1, HEADS // 2) as r:
                for p in range(2):
                    h = 2 * r + p
                    head_q(h, p, False)
                    scores(h - 1, 1 - p)
                    head_k(h, p, False)
                    outputs(h - 1, 1 - p)
            scores(HEADS - 1, 1)
            outputs(HEADS - 1, 1)

            def turn_retention(q):
                if q != 2:
                    return
                for h in range(HEADS):
                    pe.wait_ge(ret_done, h + 1)
                    if h >= 3:
                        pe.wait_ge(ret_copied, h - 2)
                    for t in range(TT):
                        mm = pe.transpose(bank(4 + h % 3)[:, P * t:P * t + P],
                                          vg[:, t, 1024 + P * h:1024 + P * h + P], ident[:, :])
                    mm.then_inc(ret_tr, 1)
                pe.wait_ge(ret_copied, HEADS)

            mix_order = list(range(HEADS, KT)) + list(range(HEADS))
            moving_group(0, mixT, mix_order, U_OUT, mix_bank_done, None, turn_retention)
            with pe.Fori(1, 4) as c:
                moving_group(c, mixT, mix_order, U_OUT, mix_bank_done,
                             lambda t: (mix_added, TT * (c - 1) + t + 1))

            pe.wait_ge(ln1_normed, TT)
            for k in range(KT):
                if k >= 8:
                    pe.wait_ge(h_copied, k - 7)
                for t in range(TT):
                    mm = pe.transpose(bank(k % 8)[:, P * t:P * t + P], h_tok[:, t, P * k:P * k + P],
                                      ident[:, :])
                mm.then_inc(h_tr, 1)
            pe.wait_ge(h_copied, KT)

            def queries(n, p, slot, r, first):
                pe.wait_ge(w_landed[slot], 16 * (U_PQ // 4 + r + 1))
                if not first:
                    pe.wait_ge(qp_copied, n - 1)
                stationary_unit(bank(p), slot, hT)

            def key_scores(n, p, first):
                pe.wait_ge(qp_copied, n + 1)
                if not first:
                    pe.wait_ge(keys_copied, n - 1)
                for t in range(TT):
                    mm = pe.matmul(bank(2 + p)[:, P * t:P * t + P], qpT[p][:, P * t:P * t + P],
                                   sub_sb[:, bass.ds(n, 1), :].rearrange("p a k -> p (a k)"),
                                   start=True, stop=True)
                mm.then_inc(key_mm, 1)

            pe.wait_ge(sub_landed, 16)
            for n in range(4):
                queries(n, n % 2, n, 0, n < 2)
                if n:
                    key_scores(n - 1, (n - 1) % 2, n < 3)
            with pe.Fori(1, 4) as r:
                for m in range(4):
                    n = 4 * r + m
                    queries(n, m % 2, m, r, False)
                    key_scores(n - 1, (m - 1) % 2, False)
            key_scores(15, 1, False)

            pe.wait_ge(keys_copied, 2 * HEADS)
            with pe.Fori(0, CHUNKS // 2) as r:
                for b in range(2):
                    c = 2 * r + b
                    for q in range(4):
                        pe.wait_ge(w_landed[q], 16 * (U_PEER // NW + c + 1))
                        ut = wslot[q].rearrange("p (k n) -> p k n", n=COLS)
                        for t in range(DENSE):
                            if q == 0:
                                pe.wait_ge(score_copied, DENSE * c + t + 1)
                            for k in range(4):
                                mm = pe.matmul(bank(DENSE * b + t), hT[:, 4 * q + k, P * (t + 1):P * (t + 2)],
                                               ut[:, k, :], start=(q == 0 and k == 0), stop=(q == 3 and k == 3))
                            if q == 3:
                                mm.then_inc(score_bank_done, 1)
                        if q < 3:
                            mm.then_inc(units_done, 1)
                        else:
                            pe.drain().then_inc(units_done, 1)


_OUT_SHAPE = (1, SEQ, D)


def _constants():
    import numpy as np
    half = P // 2
    freq = (10000.0 ** (-(np.arange(half, dtype=np.float32)) / np.float32(half))).astype(np.float32)
    m = np.arange(P)[:, None]
    c = np.arange(SEQ)[None, :]
    same, later = c // CHUNK == m // CHUNK, c // CHUNK > m // CHUNK
    gap = np.where(same, np.abs(c - m), c - m).astype(np.float64)
    decay = np.zeros((P, HEADS, SEQ), np.float32)
    for h in range(HEADS):
        gamma = 1.0 - 2.0 ** (-5.0 - h)
        decay[:, h, :] = np.where(same | later, gamma ** np.maximum(gap, 0.0), 0.0) * P ** -0.5
    return {
        "ident_c": np.eye(P, dtype=np.float32),
        "decay_c": decay,
        "freq_c": np.concatenate([freq, freq])[:, None],
        "base_c": ((np.clip(np.arange(TT * HEADS + 1) // HEADS - 1, 0, DENSE - 1) * P)[None, :]
                   + np.arange(P)[:, None]).astype(np.float32) * EXPERTS,
        "iota_c": np.tile(np.arange(K, dtype=np.float32), (P, 1)),
    }


def _stationary(wt, columns):
    return wt[:, columns].reshape(KT, P, -1, P).transpose(2, 1, 0, 3).reshape(-1, P, KT * P)


def _moving(wt, order):
    t = wt.reshape(KT, P, -1, COLS)[order]
    return t.reshape(4, 4, P, -1, COLS).transpose(3, 0, 2, 1, 4).reshape(-1, P, 4 * COLS)


def kernel(x, positions, w_in, w_out, conv_w, conv_b, w_ra, b_ra, w_ri, b_ri, lru_lambda,
           ln1_g, ln1_b, w_pq, sub_keys, peer_u, peer_v, ln2_g, ln2_b):
    import numpy as np
    import concourse.bacc as bacc
    from concourse.bass_utils import run_bass_kernel_spmd

    x, w_in, w_out, w_pq = np.asarray(x)[0], np.asarray(w_in)[0], np.asarray(w_out)[0], np.asarray(w_pq)[0]

    def turns(a, b):
        return np.concatenate([np.r_[s + P * n:s + P * n + P] for n in range(HEADS) for s in (a, b)])

    natural = list(range(KT))
    units = np.concatenate([
        _moving(w_in[:, 2048:4096], natural),
        _stationary(w_in, turns(4096, 5120)),
        _stationary(w_in, turns(0, 1024)),
        _moving(w_out, natural[HEADS:] + natural[:HEADS]),
        _stationary(w_pq, slice(None)),
    ])
    per_channel = [np.asarray(conv_w)[0][n] for n in range(4)] + [
        np.asarray(a)[0] for a in (conv_b, b_ra, b_ri, lru_lambda)]
    arrays = {
        "x_tok": np.ascontiguousarray(x.reshape(TT, P, D).transpose(1, 0, 2)),
        "x_t": np.ascontiguousarray(x.T.reshape(4, 4, P, SEQ).transpose(0, 2, 1, 3)),
        "positions": np.ascontiguousarray(positions),
        "w_units": np.ascontiguousarray(units),
        "u_units": np.ascontiguousarray(_moving(np.asarray(peer_u)[0].T, natural)),
        "gate_w": np.ascontiguousarray(np.stack([np.asarray(w_ra)[0], np.asarray(w_ri)[0]], 1)
                                       .transpose(0, 2, 1, 3)),
        "chan": np.ascontiguousarray(np.stack(per_channel).reshape(8, HEADS, P).transpose(2, 0, 1)),
        "sub_t": np.ascontiguousarray(np.asarray(sub_keys)[0].reshape(KT, NKEYS, P).transpose(2, 0, 1)),
        "ln1_t": np.ascontiguousarray(np.stack([np.asarray(ln1_g)[0], np.asarray(ln1_b)[0]])
                                      .reshape(2, KT, P).transpose(2, 0, 1)),
        "ln_rows": np.ascontiguousarray(np.concatenate([np.asarray(a) for a in (ln1_g, ln1_b, ln2_g, ln2_b)])),
        "peer_u": np.ascontiguousarray(np.asarray(peer_u)[0]),
        "peer_v": np.ascontiguousarray(np.asarray(peer_v)[0]),
        **_constants(),
    }
    nc = bacc.Bacc("TRN2", target_bir_lowering=False, num_devices=1)
    aps = {n: nc.dram_tensor(n, a.shape, mybir.dt.from_np(a.dtype), kind="ExternalInput").ap()
           for n, a in arrays.items()}
    out = nc.dram_tensor("out", _OUT_SHAPE, F32, kind="ExternalOutput").ap()
    build(nc, out=out, **aps)
    result = run_bass_kernel_spmd(nc, [arrays], core_ids=[0])
    return result.results[0]["out"]
```

```python
from contextlib import ExitStack

import concourse.bass as bass
from concourse import mybir

F32 = mybir.dt.float32
F32R = mybir.dt.float32r
I32 = mybir.dt.int32
U32 = mybir.dt.uint32
ALU = mybir.AluOpType
ACT = mybir.ActivationFunctionType
AX = mybir.AxisListType

P = 128
SEQ = 512
D = 2048
TT = SEQ // P
KT = D // P
HEADS = 8
CHUNK = 64
K = 16
NKEYS = 128
NW = 4
HALF = D // 2
BANK = 512
COLS = 512
NG = 8
NG1 = 4
EXPERTS = NKEYS * NKEYS
CHUNKS = EXPERTS // COLS
DENSE = TT - 1
ALPHA = 2.0 ** 0.25
LN_EPS = 1e-5
GN_EPS = 1e-6
LRU_C = 8.0
NEG = -3.0e38
ROUND = 1.5 * 2.0 ** 23

U_VG, U_LRU, U_QK, U_OUT, U_PQ, U_PEER = 0, 16, 32, 48, 64, 80
U_END = U_PEER + NW * CHUNKS


def two_pi_parts():
    import math
    parts, rest = [], 2 * math.pi
    for n in range(4):
        step = 2.0 ** (-9 - 12 * n)
        part = float(int(rest / step)) * step if n < 3 else rest
        parts.append(part)
        rest -= part
    return parts


def build(nc, x_tok, x_t, positions, w_units, u_units, gate_w, chan, sub_t, ln1_t, ln_rows, peer_u, peer_v,
          ident_c, decay_c, freq_c, iota_c, base_c, out):
    ctx = ExitStack()
    with ctx:
        def sb(name, shape, dt=F32):
            return ctx.enter_context(nc.sbuf_tensor(name, shape, dt))

        def place():
            return -(-nc.sbuf_base // 32) * 32

        def sem(name):
            return ctx.enter_context(nc.semaphore(name))

        big_at = place()
        big = sb("big", [P, 2 * KT * SEQ + 2 * NKEYS])
        ring_at = place()
        ring = sb("ring", [P, NG, D])
        vg = sb("vg", [P, TT, D])
        rows = sb("rows", [P, 2, D])
        work = sb("work", [P, 10 * BANK])
        mid = sb("mid", [P, 4 * BANK])
        ident = sb("ident", [P, P])
        iota = sb("iota", [P, K])
        chan_sb = sb("chan_sb", [P, 8, HEADS])
        c8 = sb("c8", [P, HEADS])
        small = sb("small", [P, 128])
        topk = sb("topk", [P, 260])
        freq = sb("freq", [P, 1])
        base = sb("base", [P, TT * HEADS + 1])
        ln1_col = sb("ln1_col", [P, 2, KT])

        src_high = nc.alloc_sbuf_tensor_at("src_high", [P, KT, SEQ], F32R, offset=big_at)
        src_low = nc.alloc_sbuf_tensor_at("src_low", [P, KT, SEQ], F32R, offset=big_at + 4 * KT * SEQ)
        w_high = nc.alloc_sbuf_tensor_at("w_high", [P, 2, HALF], F32R, offset=ring_at + 4 * 2 * D)
        w_low = nc.alloc_sbuf_tensor_at("w_low", [P, 2, HALF], F32R, offset=ring_at + 4 * 3 * D)
        x_raw = vg[:, :, :].rearrange("p t d -> p (t d)").rearrange("p (k t) -> p k t", k=KT)
        h_tok = vg
        keys_flat = big[:, KT * SEQ:2 * KT * SEQ + 2 * NKEYS]
        keys = keys_flat.rearrange("p (g n) -> p g n", n=2 * NKEYS)
        keys_at_first = [ring[:, 0:2, :].rearrange("p s d -> p (s d)"), work[:, 2 * BANK:10 * BANK]]
        hT_flat = big[:, 0:KT * SEQ]
        hT = hT_flat.rearrange("p (k t) -> p k t", k=KT)
        raw_h = ring[:, 0:2, :].rearrange("p s d -> p (s d)").rearrange("p (k t) -> p k t", k=8)
        lru_mix = ring[:, 0:2, :].rearrange("p s d -> p (s d)").rearrange("p (k t) -> p k t", k=HEADS)
        wslot = [ring[:, NG - NW + s, :] for s in range(NW)]
        decay = rows[:, :, :].rearrange("p a d -> p (a d)").rearrange("p (h t) -> p h t", h=HEADS)
        w = [work[:, n * BANK:(n + 1) * BANK] for n in range(10)]
        cosT, sinT = mid[:, 0:BANK], mid[:, BANK:2 * BANK]
        sub_sb = mid[:, :].rearrange("p (n k) -> p n k", k=NKEYS)
        wgate = mid[:, 2 * BANK:3 * BANK].rearrange("p (b a n) -> p b a n", b=2, a=2)
        xc = [w[0], w[1]]
        rgate, igate, a_t, th, gelu_gr, den, s_in, hscan = w[2], w[3], w[4], w[5], w[6], w[7], w[8], w[9]
        qT, kT, rot = [w[0], w[1]], [w[2], w[3]], [w[4], w[5]]
        probs = work[:, 6 * BANK:10 * BANK].rearrange("p (i t) -> p i t", i=TT)
        normed = mid[:, 2 * BANK:3 * BANK].rearrange("p (c e) -> p c e", c=TT)
        qpT = [w[0], w[1]]
        score_st = work[:, 0:3072].rearrange("p (b t e) -> p b t e", b=2, t=DENSE)
        s_cp, s_low = work[:, 3072:3328], mid[:, 1296:1552]
        cand, cand_low = work[:, 3456:3712], work[:, 3712:3968]
        eidx = work[:, 3968:4496].bitcast(U32)
        vidx = work[:, 4496:5024].bitcast(U32)
        gates = mid[:, 768:1296]
        extra = [keys_flat[:, n * D:(n + 1) * D] for n in range(NG1)]
        acc0 = rows[:, 0, :]
        rows2 = hT_flat[:, 0:2 * D].rearrange("p (a d) -> p a d", a=2)
        pick1 = mid[:, 0:256].rearrange("p (k j) -> p k j", j=K)
        pick2 = mid[:, 256:512].rearrange("p (k j) -> p k j", j=K)
        act_u = mid[:, 512:544].rearrange("p (b j) -> p b j", b=2)
        act_g = mid[:, 544:560]
        wgt = mid[:, 560:576]
        eidx_st = mid[:, 576:608].bitcast(U32).rearrange("p (b j) -> p b j", b=2)
        vidx_st = mid[:, 608:640].bitcast(U32).rearrange("p (b j) -> p b j", b=2)
        v1, v2 = topk[:, 0:16], topk[:, 16:32]
        i1, i2, ci = topk[:, 32:48].bitcast(U32), topk[:, 48:64].bitcast(U32), topk[:, 64:80].bitcast(U32)
        i1f, i2f = topk[:, 80:96], topk[:, 96:112]
        vs = topk[:, 112:128]
        c1, c2 = topk[:, 128:144].bitcast(U32), topk[:, 144:160].bitcast(U32)
        c1f, c2f, e1, e2 = (topk[:, 160 + 16 * n:176 + 16 * n] for n in range(4))
        less, expo = topk[:, 224:240], topk[:, 240:256]
        ssum, rsum = topk[:, 256:257], topk[:, 257:258]
        stats = small[:, 0:96].rearrange("p (t c s) -> p t c s", t=TT, c=4)
        mv = small[:, 96:104].rearrange("p (t s) -> p t s", t=TT)
        sd, rstd = small[:, 104:108], small[:, 108:112]
        lam = [small[:, 8 * n:8 * n + 8] for n in range(8)]
        ang, turns, hi_turns, prod = w[2], w[3], w[4], w[5]
        pos_i = work[:, 3072:3584].bitcast(I32)

        psum = ctx.enter_context(nc.psum_tensor("psum", [P, 8, BANK], F32))

        def bank(n):
            return psum[:, n, :]

        x_landed = [sem(f"x_landed{n}") for n in range(4)]
        x_landed_early = sem("x_landed_early")
        w_landed_early = sem("w_landed_early")
        w_landed = [sem(f"w_landed{n}") for n in range(NW)]
        consts_landed = sem("consts_landed")
        decay_landed = sem("decay_landed")
        tok_landed0 = sem("tok_landed0")
        tok_landed = sem("tok_landed")
        gate_landed = [sem("gate_landed0"), sem("gate_landed1")]
        rows_landed = sem("rows_landed")
        rows2_landed = sem("rows2_landed")
        sub_landed = sem("sub_landed")
        x_high = sem("x_high")
        x_split = sem("x_split")
        halves_split = sem("halves_split")
        half_seen_free = sem("half_seen_free")
        mix_high = sem("mix_high")
        mix_split = sem("mix_split")
        halves_done = sem("halves_done")
        vg_bank_done = sem("vg_bank_done")
        vg_bank_free = sem("vg_bank_free")
        lam_ready = sem("lam_ready")
        c8_ready = sem("c8_ready")
        trig_ready = sem("trig_ready")
        sin_done = sem("sin_done")
        conv_done = sem("conv_done")
        gates_mm = sem("gates_mm")
        lru_act = sem("lru_act")
        sq_ready = sem("sq_ready")
        sq_done = sem("sq_done")
        lru_done = sem("lru_done")
        rot_q = sem("rot_q")
        rot_k = sem("rot_k")
        scores_mm = sem("scores_mm")
        masked = sem("masked")
        o_mm = sem("o_mm")
        var_ready = sem("var_ready")
        sd_ready = sem("sd_ready")
        ret_done = sem("ret_done")
        ret_tr = sem("ret_tr")
        mix_bank_done = sem("mix_bank_done")
        mix_added = sem("mix_added")
        ln1_normed = sem("ln1_normed")
        h_tr = sem("h_tr")
        h_copied = sem("h_copied")
        h_high = sem("h_high")
        h_split = sem("h_split")
        h_whole = sem("h_whole")
        keys_moved = sem("keys_moved")
        qp_copied = sem("qp_copied")
        key_mm = sem("key_mm")
        keys_copied = sem("keys_copied")
        exp_in = sem("exp_in")
        exp_out = sem("exp_out")
        extra_landed = [sem(f"extra_landed{n}") for n in range(NG1)]
        g_landed = [sem(f"g_landed{n}") for n in range(NG)]
        slot_seen_free = sem("slot_seen_free")
        u_used = sem("u_used")
        v_used = sem("v_used")
        gelu_out = sem("gelu_out")
        score_bank_done = sem("score_bank_done")
        score_copied = sem("score_copied")
        score_stored = [sem("score_stored0"), sem("score_stored1")]
        staged = sem("staged")
        staged_v = sem("staged_v")
        val_landed = [sem("val_landed0"), sem("val_landed1")]
        wgt_ready = sem("wgt_ready")
        y_ready = sem("y_ready")
        y_stored = sem("y_stored")
        products = nc.dram_tensor("products", (DENSE * P * EXPERTS, 1), F32, kind="Internal").ap()
        products_v = products.rearrange("(t p e) a -> p t (e a)", t=DENSE, e=EXPERTS)
        out_v = out.rearrange("b (t p) d -> (b t) p d", p=P)

        block = ctx.enter_context(nc.Block())

        @block.sync
        def _(sp):
            for half in range(2):
                sp.dma_start(x_raw[:, 2 * half:2 * half + 2, :], x_t[0, :, 2 * half:2 * half + 2, :]
                             ).then_inc(x_landed[0] if half else x_landed_early, 16)
                span = slice(half * HALF, (half + 1) * HALF)
                sp.dma_start(wslot[0][:, span], w_units[0, :, span]).then_inc(w_landed[0] if half else w_landed_early, 16)
            for s in range(1, NW):
                sp.dma_start(x_raw[:, 4 * s:4 * s + 4, :], x_t[s]).then_inc(x_landed[s], 16)
                sp.dma_start(wslot[s], w_units[s]).then_inc(w_landed[s], 16)
            with sp.Fori(1, U_PEER // NW) as r:
                for s in range(NW):
                    sp.wait_ge(halves_split, 2 * (NW * r + s + 1 - NW))
                    sp.dma_start(wslot[s], w_units[NW * r + s]).then_inc(w_landed[s], 16)
            for s in range(NW):
                sp.wait_ge(halves_split, 2 * (U_PEER + s + 1 - NW))
                sp.dma_start(wslot[s], u_units[s]).then_inc(w_landed[s], 16)
            with sp.Fori(1, CHUNKS) as c:
                for s in range(NW):
                    sp.wait_ge(halves_done, 2 * (U_PEER + NW * c + s + 1 - NW))
                    sp.dma_start(wslot[s], u_units[NW * c + s]).then_inc(w_landed[s], 16)
            for half in range(2):
                cols = slice(half * HALF, (half + 1) * HALF)
                sp.wait_ge(y_ready, half + 1)
                sp.dma_start(out_v[0, :, cols], acc0[:, cols]).then_inc(y_stored, 16)
            with sp.Fori(1, TT) as t:
                for half in range(2):
                    cols = slice(half * HALF, (half + 1) * HALF)
                    sp.wait_ge(y_ready, 2 * t + half + 1)
                    sp.dma_start(out_v[bass.ds(t, 1), :, cols].rearrange("a p d -> p (a d)"),
                                 h_tok[:, bass.ds(t, 1), cols].rearrange("p a d -> p (a d)")
                                 ).then_inc(y_stored, 16)
            sp.wait_ge(y_stored, 16 * 2 * TT)

        @block.scalar
        def _(act):
            for n in range(8):
                act.wait_ge(x_landed[n // 2] if n else x_landed_early, 16)
                act.activation(src_high[:, 2 * n:2 * n + 2, :], x_raw[:, 2 * n:2 * n + 2, :], ACT.Copy
                               ).then_inc(x_high, 1)
            act.dma_start(chan_sb[:, :, :], chan).then_inc(consts_landed, 16)
            act.dma_start(freq[:, :], freq_c).then_inc(consts_landed, 16)
            act.dma_start(pos_i, positions.partition_broadcast(P)).then_inc(consts_landed, 16)
            act.dma_start(ident[:, :], ident_c).then_inc(consts_landed, 16)
            act.dma_start(iota[:, :], iota_c).then_inc(consts_landed, 16)
            act.dma_start(ln1_col[:, :, :], ln1_t).then_inc(consts_landed, 16)
            act.dma_start(base[:, :], base_c).then_inc(consts_landed, 16)
            for p in range(2):
                act.dma_start(wgate[:, p, :, :], gate_w[p]).then_inc(gate_landed[p], 16)
            act.wait_ge(lam_ready, 1)
            act.activation(lam[2], lam[1], ACT.Exp, scale=-1.0).then_inc(lam_ready, 1)
            act.wait_ge(trig_ready, 1)
            act.activation(sinT, sinT, ACT.Sin).then_inc(sin_done, 1)
            act.activation(cosT, cosT, ACT.Sin).then_inc(sin_done, 1)
            for g in range(4):
                if g == 1:
                    act.dma_start(decay, decay_c).then_inc(decay_landed, 16)
                for t in range(TT):
                    act.wait_ge(vg_bank_done, TT * g + t + 1)
                    act.activation(vg[:, t, g * COLS:(g + 1) * COLS], bank(t),
                                   ACT.Copy if g < 2 else ACT.Silu).then_inc(vg_bank_free, 1)

            def load_gates(g, p):
                act.dma_start(wgate[:, p, :, :], gate_w[g]).then_inc(gate_landed[p], 16)

            def lru(g, p, more=True):
                act.wait_ge(gates_mm, g + 1)
                if more:
                    load_gates(g + 2, p)
                if not isinstance(g, int) or g >= 1:
                    act.wait_ge(lru_done, g)
                act.activation(rgate, bank(4 * p + 2), ACT.Sigmoid, bias=chan_sb[:, 5, bass.ds(g, 1)])
                act.activation(igate, bank(4 * p + 3), ACT.Sigmoid, bias=chan_sb[:, 6, bass.ds(g, 1)])
                act.drain()
                act.activation(a_t, rgate, ACT.Exp, scale=c8[:, bass.ds(g, 1)])
                act.activation(th, rgate, ACT.Tanh, scale=c8[:, bass.ds(g, 1)]).then_inc(lru_act, 1)
                act.wait_ge(halves_done, 2 * (U_LRU + 2 * g + 2))
                act.activation(gelu_gr, bank(4 * p + 1), ACT.Gelu_apprx_tanh).then_inc(lru_act, 1)
                act.wait_ge(sq_ready, g + 1)
                act.activation(s_in, s_in, ACT.Sqrt).then_inc(sq_done, 1)

            act.wait_ge(c8_ready, 1)
            lru(0, 0)
            lru(1, 1)
            with act.Fori(1, HEADS // 2 - 1) as r:
                for p in range(2):
                    lru(2 * r + p, p)
            lru(HEADS - 2, 0, False)
            lru(HEADS - 1, 1, False)
            with act.Fori(0, HEADS - 1) as h:
                act.wait_ge(var_ready, h + 1)
                act.activation(sd, sd, ACT.Sqrt).then_inc(sd_ready, 1)
            act.wait_ge(halves_done, 2 * U_OUT)
            for n in range(HEADS):
                act.activation(src_high[:, HEADS + n, :], lru_mix[:, n, :], ACT.Copy).then_inc(mix_high, 1)
            act.wait_ge(var_ready, HEADS)
            act.activation(sd, sd, ACT.Sqrt).then_inc(sd_ready, 1)
            for h in range(HEADS):
                act.wait_ge(ret_tr, h + 1)
                act.activation(src_high[:, h, :], bank(4 + h % 3), ACT.Copy).then_inc(mix_high, 1)
            for c in range(4):
                act.dma_start(h_tok[:, :, c * COLS:(c + 1) * COLS], x_tok[:, :, c * COLS:(c + 1) * COLS]
                              ).then_inc(tok_landed if c else tok_landed0, 16)
            act.wait_ge(masked, TT * HEADS)
            act.dma_start(rows[:, :, :], ln_rows[0:2].partition_broadcast(P)).then_inc(rows_landed, 16)
            act.wait_ge(ret_done, HEADS)
            act.dma_start(sub_sb, sub_t).then_inc(sub_landed, 16)
            act.wait_ge(var_ready, HEADS + 1)
            act.activation(sd, sd, ACT.Sqrt).then_inc(sd_ready, 1)
            for k in range(KT):
                act.wait_ge(h_tr, k + 1)
                if k >= 8:
                    act.wait_ge(h_split, k - 7)
                act.activation(raw_h[:, k % 8, :], bank(k % 8), ACT.Identity, bias=ln1_col[:, 1, k:k + 1],
                               scale=ln1_col[:, 0, k:k + 1]).then_inc(h_copied, 1)
            def peer_q(n, p):
                act.wait_ge(halves_done, 2 * (U_PQ + n + 1))
                if not isinstance(n, int) or n >= 2:
                    act.wait_ge(key_mm, n - 1)
                act.activation(qpT[p], bank(p), ACT.Copy).then_inc(qp_copied, 1)

            def peer_s(n, p):
                act.wait_ge(key_mm, n + 1)
                for half in range(2):
                    by_unit = keys_at_first[half].rearrange("p (t m n) -> p t m n", t=2, n=NKEYS)
                    act.activation(by_unit[:, :, bass.ds(n, 1), :].rearrange("p t a n -> p t (a n)"),
                                   bank(2 + p)[:, 2 * half * P:2 * (half + 1) * P].rearrange("p (t n) -> p t n", t=2),
                                   ACT.Copy).then_inc(keys_copied, 1)

            for n in range(4):
                peer_q(n, n % 2)
                if n:
                    peer_s(n - 1, (n - 1) % 2)
            with act.Fori(1, 4) as r:
                for m in range(4):
                    peer_q(4 * r + m, m % 2)
                    peer_s(4 * r + m - 1, (m - 1) % 2)
            peer_s(15, 1)
            act.sem_inc(score_copied, 2 * DENSE)
            act.wait_ge(h_whole, KT)
            act.wait_ge(keys_copied, 4 * HEADS)
            for n in range(4):
                act.activation(keys_flat[:, n * D:(n + 1) * D], keys_at_first[n // 2][:, n % 2 * D:(n % 2 + 1) * D],
                               ACT.Copy).then_inc(keys_moved, 1)
            act.wait_ge(keys_moved, 4)

            def softmax(g):
                act.wait_ge(exp_in, g + 1)
                act.activation(expo, less, ACT.Exp, accum_out=ssum).then_inc(exp_out, 1)

            def chunk(c, b, first):
                if not first:
                    act.wait_ge(score_stored[b], 8 * (c - b))
                for t in range(DENSE):
                    act.wait_ge(score_bank_done, DENSE * c + t + 1)
                    act.activation(score_st[:, b, t, :], bank(DENSE * b + t), ACT.Copy).then_inc(score_copied, 1)
                act.wait_ge(score_copied, DENSE * (c + 1) + 2 * DENSE)
                act.dma_start(products_v[:, :, bass.ds(c * COLS, COLS)], score_st[:, b, :, :]
                              ).then_inc(score_stored[b], 16)

            def sparse_group(h, first):
                softmax(4 * h + 1)
                chunk(4 * h, 0, first)
                act.wait_ge(u_used, h * K + K)
                act.activation(act_g, act_u[:, 0, :], ACT.Gelu_apprx_tanh).then_inc(gelu_out, 1)
                softmax(4 * h + 2)
                chunk(4 * h + 1, 1, first)
                softmax(4 * h + 3)
                chunk(4 * h + 2, 0, False)
                softmax(4 * h + 4)
                chunk(4 * h + 3, 1, False)

            softmax(0)
            sparse_group(0, True)
            with act.Fori(1, HEADS) as h:
                sparse_group(h, False)
            act.wait_ge(halves_done, 2 * U_END)
            act.dma_start(rows2, ln_rows[2:4].partition_broadcast(P)).then_inc(rows2_landed, 16)

            def ln2_sd(t):
                act.wait_ge(var_ready, HEADS + 2 + t)
                act.activation(sd[:, 0:1], sd[:, 0:1], ACT.Sqrt).then_inc(sd_ready, 1)

            ln2_sd(0)
            with act.Fori(1, TT) as t:
                with act.Fori(0, HEADS // 2) as hp:
                    for par in range(2):
                        g = HEADS * t + 2 * hp + par
                        act.wait_ge(val_landed[par], 16 * K * (4 * (t - 1) + hp + 1))
                        act.wait_ge(wgt_ready, g)
                        act.activation(act_g, act_u[:, par, :], ACT.Gelu_apprx_tanh).then_inc(gelu_out, 1)
                ln2_sd(t)

        @block.gpsimd
        def _(pool):
            def split_unit(r, s):
                for half in range(2):
                    n = 2 * (NW * r + s) + half
                    if isinstance(n, int) and n == 0:
                        pool.wait_ge(w_landed_early, 16)
                    elif half == 0 or (isinstance(n, int) and n == 1):
                        pool.wait_ge(w_landed[s], 16 * (r + 1))
                    if not isinstance(n, int) or n >= 2:
                        pool.wait_ge(halves_done, n - 1)
                    raw = wslot[s][:, half * HALF:(half + 1) * HALF]
                    pool.sem_inc(half_seen_free, 1)
                    pool.tensor_scalar(w_high[:, half, :], raw, 1.0, 0.0, ALU.mult, ALU.add)
                    pool.drain()
                    pool.tensor_tensor(w_low[:, half, :], raw, w_high[:, half, :].bitcast(F32), ALU.subtract
                                       ).then_inc(halves_split, 1)

            for s in range(NW):
                split_unit(0, s)
            with pool.Fori(1, U_PEER // NW) as r:
                for s in range(NW):
                    split_unit(r, s)

            def gather(dst, table, idx, landed):
                pool.sem_inc(slot_seen_free, 1)
                pool.indirect_dma_start(dst, None, table, bass.IndirectOffsetOnAxis(idx, 0)
                                        ).then_inc(landed, 16)

            def first_tile_v(g):
                for j in range(K):
                    s = j % NG1
                    if j < NG1:
                        pool.wait_ge(u_used, K * g + K - NG1 + j + 1)
                    else:
                        pool.wait_ge(v_used, K * g + j - NG1 + 1)
                    gather(ring[:, s, :], peer_v, eidx_st[:, 1, j:j + 1], g_landed[s])

            def first_tile_u(g, first):
                for j in range(K):
                    s = j % NG1
                    if j >= NG1:
                        pool.wait_ge(u_used, K * g + j - NG1 + 1)
                    elif not first:
                        pool.wait_ge(v_used, K * g - NG1 + j + 1)
                    gather(ring[:, s, :], peer_u, eidx_st[:, 0, j:j + 1], g_landed[s])

            pool.wait_ge(staged, 1)
            first_tile_u(0, True)
            with pool.Fori(1, HEADS) as g:
                pool.wait_ge(staged_v, g)
                first_tile_v(g - 1)
                pool.wait_ge(staged, g + 1)
                first_tile_u(g, False)
            pool.wait_ge(staged_v, HEADS)
            first_tile_v(HEADS - 1)
            def picked_products(par):
                for j in range(K):
                    gather(act_u[:, par, j:j + 1], products, vidx_st[:, par, j:j + 1], val_landed[par])

            def rows_of_v(g, par, js, first=False):
                for j in js:
                    s = j % NG
                    if not first:
                        pool.wait_ge(v_used, K * g + j - NG + 1)
                    gather(ring[:, s, :], peer_v, eidx_st[:, par, j:j + 1], g_landed[s])

            def group(g, par):
                pool.wait_ge(staged, g + 2)
                picked_products(par)
                rows_of_v(g, par, range(K))

            pool.wait_ge(exp_in, TT * HEADS)
            pool.wait_ge(staged, HEADS + 1)
            for n in range(NG1):
                gather(extra[n], peer_v, eidx_st[:, 0, n:n + 1], extra_landed[n])
            pool.wait_ge(staged, HEADS + 2)
            rows_of_v(HEADS, 0, range(NG, NG + NG1), True)
            pool.wait_ge(halves_done, 2 * U_END)
            rows_of_v(HEADS, 0, range(NG1, NG), True)
            for b in range(2):
                pool.wait_ge(score_stored[b], 16 * CHUNKS // 2)
            picked_products(0)
            for n in range(NG1):
                j = NG + NG1 + n
                pool.wait_ge(v_used, K * HEADS + n + 1)
                gather(extra[n], peer_v, eidx_st[:, 0, j:j + 1], extra_landed[n])
            group(HEADS + 1, 1)
            with pool.Fori(HEADS // 2 + 1, TT * HEADS // 2) as r:
                for par in range(2):
                    group(2 * r + par, par)

        @block.vector
        def _(dve):
            for n in range(8):
                k = slice(2 * n, 2 * n + 2)
                dve.wait_ge(x_high, n + 1)
                dve.tensor_tensor(src_low[:, k, :], x_raw[:, k, :], src_high[:, k, :].bitcast(F32), ALU.subtract
                                  ).then_inc(x_split, 1)
            dve.wait_ge(consts_landed, 16 * 7)
            lam_in = chan_sb[:, 7, :]
            dve.scalar_tensor_tensor(out=lam[1], in0=lam_in, scalar=-1.0, in1=lam_in, op0=ALU.mult, op1=ALU.max).then_inc(lam_ready, 1)
            dve.wait_ge(lam_ready, 2)
            dve.tensor_scalar(lam[3], lam[2], 2.0, None, ALU.add)
            dve.drain()
            dve.reciprocal(lam[4], lam[3])
            dve.drain()
            dve.tensor_tensor(lam[3], lam[2], lam[4], ALU.mult)
            dve.drain()
            dve.tensor_tensor(lam[4], lam[3], lam[3], ALU.mult)
            dve.drain()
            dve.tensor_scalar(lam[5], lam[4], 1.0 / 19, None, ALU.mult)
            dve.drain()
            for n in range(8, 0, -1):
                a, b = (5, 6) if n % 2 == 0 else (6, 5)
                dve.scalar_tensor_tensor(out=lam[b], in0=lam[a], scalar=1.0 / (2 * n + 1), in1=lam[4],
                                         op0=ALU.add, op1=ALU.mult)
                dve.drain()
            dve.tensor_scalar(lam[6], lam[5], 1.0, 2.0, ALU.add, ALU.mult)
            dve.tensor_scalar(lam[2], lam_in, 0.0, None, ALU.min)
            dve.drain()
            dve.tensor_tensor(lam[7], lam[6], lam[3], ALU.mult)
            dve.drain()
            dve.tensor_tensor(lam[6], lam[2], lam[7], ALU.subtract)
            dve.drain()
            dve.tensor_scalar(c8[:, :], lam[6], LRU_C, None, ALU.mult).then_inc(c8_ready, 1)
            dve.tensor_copy(ang, pos_i)
            dve.drain()
            dve.tensor_scalar(ang, ang, freq[:, 0:1], None, ALU.mult)
            dve.drain()
            dve.tensor_scalar(turns, ang, 0.15915494309189535, ROUND, ALU.mult, ALU.add)
            dve.drain()
            dve.tensor_scalar(turns, turns, -ROUND, None, ALU.add)
            dve.drain()
            dve.tensor_scalar(hi_turns, turns, 2.0 ** -11, ROUND, ALU.mult, ALU.add)
            dve.drain()
            dve.tensor_scalar(hi_turns, hi_turns, -ROUND, 2.0 ** 11, ALU.add, ALU.mult)
            dve.drain()
            dve.tensor_tensor(turns, turns, hi_turns, ALU.subtract)
            dve.drain()
            for part in two_pi_parts():
                for n in (hi_turns, turns):
                    dve.scalar_tensor_tensor(out=ang, in0=n, scalar=-part, in1=ang, op0=ALU.mult,
                                             op1=ALU.add)
                    dve.drain()
            dve.tensor_scalar(ang, ang, 3.1415925, -3.1415925, ALU.min, ALU.max)
            dve.drain()
            dve.tensor_scalar(sinT[0:64], ang[0:64], 1.0, None, ALU.mult)
            dve.tensor_scalar(sinT[64:128], ang[64:128], -1.0, None, ALU.mult)
            dve.scalar_tensor_tensor(out=prod, in0=ang, scalar=-1.0, in1=ang, op0=ALU.mult, op1=ALU.max)
            dve.drain()
            dve.tensor_scalar(cosT, prod, -1.0, 1.5707963267948966, ALU.mult, ALU.add).then_inc(trig_ready, 1)
            dve.wait_ge(sin_done, 2)

            def conv(g, p):
                dve.wait_ge(halves_done, 2 * (U_LRU + 2 * g + 1))
                src = bank(4 * p)

                def tap(n):
                    return chan_sb[:, n, bass.ds(g, 1)]
                dve.tensor_scalar(xc[p], src, tap(3), tap(4), ALU.mult, ALU.add)
                for back in range(1, 4):
                    dve.drain()
                    last = dve.scalar_tensor_tensor(out=xc[p][:, back:SEQ], in0=src[:, 0:SEQ - back],
                                                    scalar=tap(3 - back), in1=xc[p][:, back:SEQ],
                                                    op0=ALU.mult, op1=ALU.add)
                last.then_inc(conv_done, 1)

            def lru(g, p):
                dve.wait_ge(lru_act, 2 * g + 1)
                dve.tensor_tensor(igate, igate, xc[p], ALU.mult)
                dve.tensor_scalar(den, th, -1.0, 1.0, ALU.mult, ALU.add)
                dve.drain()
                dve.reciprocal(hscan, den)
                dve.drain()
                dve.scalar_tensor_tensor(out=s_in, in0=th, scalar=-2.0, in1=hscan, op0=ALU.mult,
                                         op1=ALU.mult).then_inc(sq_ready, 1)
                dve.wait_ge(sq_done, g + 1)
                dve.tensor_tensor(den, s_in, igate, ALU.mult)
                dve.drain()
                dve.tensor_tensor_scan(out=hscan, data0=a_t, data1=den, initial=0.0, op0=ALU.mult,
                                       op1=ALU.add)
                dve.drain()
                dve.wait_ge(lru_act, 2 * g + 2)
                dve.tensor_tensor(lru_mix[:, bass.ds(g, 1), :].rearrange("p a t -> p (a t)"),
                                  hscan, gelu_gr, ALU.mult).then_inc(lru_done, 1)
                dve.drain()

            conv(0, 0)
            conv(1, 1)
            lru(0, 0)
            with dve.Fori(1, HEADS // 2) as r:
                conv(2 * r, 0)
                lru(2 * r - 1, 1)
                conv(2 * r + 1, 1)
                lru(2 * r, 0)
            lru(HEADS - 1, 1)

            def rotate(src, dst, done):
                dve.tensor_tensor(rot[0], src, cosT, ALU.mult)
                dve.tensor_tensor(rot[1][0:64], src[64:128], sinT[64:128], ALU.mult)
                dve.tensor_tensor(rot[1][64:128], src[0:64], sinT[0:64], ALU.mult)
                dve.drain()
                dve.tensor_tensor(dst, rot[0], rot[1], ALU.add).then_inc(done, 1)
                dve.drain()

            def rotate_q(h, p):
                dve.wait_ge(halves_done, 2 * (U_QK + 2 * h + 1))
                rotate(bank(p), qT[p], rot_q)

            def rotate_k(h, p):
                dve.wait_ge(halves_done, 2 * (U_QK + 2 * h + 2))
                rotate(bank(2 + p), kT[p], rot_k)

            def mask(h):
                for i in range(TT):
                    n = SEQ - P * i
                    dve.wait_ge(scores_mm, TT * h + i + 1)
                    dve.tensor_tensor(probs[:, i, 0:n], bank(4 + i % 2)[:, 0:n],
                                      decay[:, bass.ds(h, 1), 0:n].rearrange("p a t -> p (a t)"),
                                      ALU.mult).then_inc(masked, 1)

            def group_norm(h, p):
                dve.wait_ge(o_mm, h + 1)
                o = bank(6 + p).rearrange("p (c e) -> p c e", c=TT)
                for c in range(TT):
                    dve.bn_stats(stats[:, c, 0, :], o[:, c, :])
                dve.drain()
                for c in range(TT):
                    dve.bn_aggr(mv[:, c, :], stats[:, c, 0, :])
                dve.drain()
                dve.tensor_scalar(sd, mv[:, :, 1], GN_EPS, None, ALU.add).then_inc(var_ready, 1)
                dve.wait_ge(sd_ready, h + 1)
                dve.reciprocal(rstd, sd)
                dve.drain()
                for c in range(TT):
                    dve.tensor_scalar(normed[:, c, :], o[:, c, :], mv[:, c, 0:1], rstd[:, c:c + 1],
                                      ALU.subtract, ALU.mult)
                dve.drain()
                gate = vg[:, :, bass.ds(1024 + P * h, P)]
                dve.tensor_tensor(gate, normed, gate, ALU.mult).then_inc(ret_done, 1)
                dve.drain()

            dve.wait_ge(decay_landed, 16)
            rotate_q(0, 0)
            rotate_k(0, 0)
            rotate_q(1, 1)
            mask(0)
            rotate_k(1, 1)
            group_norm(0, 0)
            with dve.Fori(1, HEADS // 2) as r:
                for p in range(2):
                    h = 2 * r + p
                    mask(h - 1)
                    rotate_q(h, p)
                    rotate_k(h, p)
                    group_norm(h - 1, 1 - p)
            mask(HEADS - 1)
            for n in range(HEADS):
                dve.wait_ge(mix_high, n + 1)
                dve.tensor_tensor(src_low[:, HEADS + n, :], lru_mix[:, n, :],
                                  src_high[:, HEADS + n, :].bitcast(F32), ALU.subtract).then_inc(mix_split, 1)
            group_norm(HEADS - 1, 1)
            for h in range(HEADS):
                dve.wait_ge(mix_high, HEADS + h + 1)
                dve.tensor_tensor(src_low[:, h, :], bank(4 + h % 3), src_high[:, h, :].bitcast(F32),
                                  ALU.subtract).then_inc(mix_split, 1)

            def add_mix(c):
                for t in range(TT):
                    dve.wait_ge(mix_bank_done, TT * c + t + 1)
                    cols = h_tok[:, t, bass.ds(c * COLS, COLS)]
                    dve.scalar_tensor_tensor(out=cols, in0=cols, scalar=ALPHA, in1=bank(t), op0=ALU.mult,
                                             op1=ALU.add).then_inc(mix_added, 1)
                dve.drain()
                for t in range(TT):
                    cols = h_tok[:, t, bass.ds(c * COLS, COLS)]
                    dve.bn_stats(stats[:, t, bass.ds(c, 1), :].rearrange("p a s -> p (a s)"), cols)

            dve.wait_ge(tok_landed0, 16)
            add_mix(0)
            dve.wait_ge(tok_landed, 16 * 3)
            with dve.Fori(1, 4) as c:
                add_mix(c)
            dve.drain()
            for t in range(TT):
                dve.bn_aggr(mv[:, t, :], stats[:, t, :, :])
            dve.drain()
            dve.tensor_scalar(sd, mv[:, :, 1], LN_EPS, None, ALU.add).then_inc(var_ready, 1)
            dve.wait_ge(sd_ready, HEADS + 1)
            dve.reciprocal(rstd, sd)
            dve.drain()
            for c in range(4):
                for t in range(TT):
                    cols = h_tok[:, t, c * COLS:(c + 1) * COLS]
                    dve.tensor_scalar(cols, cols, mv[:, t, 0:1], rstd[:, t:t + 1], ALU.subtract, ALU.mult
                                      ).then_inc(ln1_normed, 1)
            for k in range(KT):
                dve.wait_ge(h_copied, k + 1)
                dve.tensor_copy(src_high[:, k, :], raw_h[:, k % 8, :]).then_inc(h_high, 1)
                dve.wait_ge(h_high, k + 1)
                dve.tensor_tensor(src_low[:, k, :], raw_h[:, k % 8, :], src_high[:, k, :].bitcast(F32),
                                  ALU.subtract).then_inc(h_split, 1)
            dve.wait_ge(rows_landed, 16)
            for t in range(TT):
                dve.drain()
                dve.tensor_tensor(h_tok[:, t, :], h_tok[:, t, :], rows[:, 0, :], ALU.mult)
                dve.drain()
                dve.tensor_tensor(h_tok[:, t, :], h_tok[:, t, :], rows[:, 1, :], ALU.add)
            dve.drain()

            def top16(*jobs):
                for vals, idx, src, low in jobs:
                    dve.max(vals[:, 0:8], src)
                dve.drain()
                for vals, idx, src, low in jobs:
                    dve.max_index(idx[:, 0:8], vals[:, 0:8], src)
                    dve.match_replace(low, vals[:, 0:8], src, NEG)
                dve.drain()
                for vals, idx, src, low in jobs:
                    dve.max(vals[:, 8:16], low)
                dve.drain()
                for vals, idx, src, low in jobs:
                    dve.max_index(idx[:, 8:16], vals[:, 8:16], low)
                dve.drain()

            def over_j(ap):
                return ap.rearrange("p (k a) -> p k a", a=1).broadcast_to([P, K, K])

            def over_k(ap):
                return ap.rearrange("p (a j) -> p a j", a=1).broadcast_to([P, K, K])

            def choose(g):
                dve.tensor_copy(s_cp, keys[:, bass.ds(g, 1), :].rearrange("p a n -> p (a n)"))
                dve.drain()
                top16((v1, i1, s_cp[:, 0:NKEYS], s_low[:, 0:NKEYS]),
                      (v2, i2, s_cp[:, NKEYS:2 * NKEYS], s_low[:, NKEYS:2 * NKEYS]))
                dve.tensor_tensor(cand.rearrange("p (k j) -> p k j", j=K), over_j(v1), over_k(v2), ALU.add)
                dve.tensor_copy(i1f, i1)
                dve.tensor_copy(i2f, i2)
                dve.drain()
                top16((vs, ci, cand, cand_low))
                dve.tensor_scalar(c1, ci, 4, None, ALU.logical_shift_right)
                dve.tensor_scalar(c2, ci, 15, None, ALU.bitwise_and)
                dve.drain()
                dve.tensor_copy(c1f, c1)
                dve.tensor_copy(c2f, c2)
                dve.drain()
                dve.tensor_tensor(pick1, over_j(c1f), over_k(iota[:, :]), ALU.is_equal)
                dve.tensor_tensor(pick2, over_j(c2f), over_k(iota[:, :]), ALU.is_equal)
                dve.drain()
                dve.tensor_tensor(pick1, pick1, over_k(i1f), ALU.mult)
                dve.tensor_tensor(pick2, pick2, over_k(i2f), ALU.mult)
                dve.drain()
                dve.tensor_reduce(e1, pick1, AX.X, ALU.add)
                dve.tensor_reduce(e2, pick2, AX.X, ALU.add)
                dve.tensor_scalar(less, vs, vs[:, 0:1], None, ALU.subtract).then_inc(exp_in, 1)
                dve.drain()
                span = bass.ds(g * K, K)
                dve.scalar_tensor_tensor(out=e1, in0=e1, scalar=float(NKEYS), in1=e2, op0=ALU.mult,
                                         op1=ALU.add)
                dve.drain()
                dve.tensor_copy(eidx[:, span], e1)
                dve.tensor_scalar(vidx[:, span], e1, base[:, bass.ds(g, 1)], None, ALU.add)
                dve.drain()
                dve.wait_ge(exp_out, g + 1)
                dve.reciprocal(rsum, ssum)
                dve.drain()
                dve.tensor_scalar(gates[:, span], expo, rsum, None, ALU.mult)
                dve.drain()

            dve.wait_ge(halves_done, 2 * U_PEER)
            for k in range(KT):
                dve.tensor_tensor(hT[:, k, P:SEQ], src_high[:, k, P:SEQ].bitcast(F32),
                                  src_low[:, k, P:SEQ].bitcast(F32), ALU.add).then_inc(h_whole, 1)
            dve.wait_ge(keys_moved, 4)
            dve.memset(keys[:, TT * HEADS, :], 0.0)
            dve.drain()
            choose(0)
            dve.tensor_scalar(acc0, h_tok[:, 0, :], ALPHA, None, ALU.mult)
            dve.drain()

            def stage(g, par):
                dve.tensor_copy(vidx_st[:, par, :], vidx[:, bass.ds(g * K, K)])
                dve.tensor_copy(eidx_st[:, par, :], eidx[:, bass.ds(g * K, K)])
                dve.drain().then_inc(staged, 1)

            def weigh(g):
                dve.wait_ge(gelu_out, g + 1)
                dve.tensor_tensor(wgt, act_g, gates[:, bass.ds(g * K, K)], ALU.mult).then_inc(wgt_ready, 1)
                dve.wait_ge(wgt_ready, g + 1)

            def add_rows(g, acc, row, js=range(K)):
                for j in js:
                    place, landed, count = row(j)
                    dve.wait_ge(landed, count)
                    if j:
                        dve.wait_ge(v_used, K * g + j)
                    dve.scalar_tensor_tensor(out=acc, in0=place, scalar=wgt[:, j:j + 1], in1=acc,
                                             op0=ALU.mult, op1=ALU.add).then_inc(v_used, 1)
                dve.wait_ge(v_used, K * g + js[-1] + 1)

            def second_ln(t, acc):
                for c in range(4):
                    dve.bn_stats(stats[:, 0, c, :], acc[:, c * BANK:(c + 1) * BANK])
                dve.drain()
                dve.bn_aggr(mv[:, 0, :], stats[:, 0, :, :])
                dve.drain()
                dve.tensor_scalar(sd[:, 0:1], mv[:, 0, 1:2], LN_EPS, None, ALU.add).then_inc(var_ready, 1)
                dve.wait_ge(sd_ready, HEADS + 2 + t)
                dve.reciprocal(rstd[:, 0:1], sd[:, 0:1])
                dve.drain()
                halves = (slice(0, HALF), slice(HALF, D))
                for cols in halves:
                    dve.scalar_tensor_tensor(out=acc[:, cols], in0=acc[:, cols], scalar=mv[:, 0, 0:1],
                                             in1=rows2[:, 0, cols], op0=ALU.subtract, op1=ALU.mult)
                dve.drain()
                for cols in halves:
                    dve.scalar_tensor_tensor(out=acc[:, cols], in0=acc[:, cols], scalar=rstd[:, 0:1],
                                             in1=rows2[:, 1, cols], op0=ALU.mult, op1=ALU.add).then_inc(y_ready, 1)

            def stage_first(g, side, signal):
                dve.tensor_copy(eidx_st[:, side, :], eidx[:, bass.ds(g * K, K)]).then_inc(signal, 1)

            def products_u(g, js):
                for j in js:
                    s = j % NG1
                    dve.wait_ge(g_landed[s], 16 * (8 * g + j // NG1 + 1))
                    dve.scalar_tensor_tensor(out=ring[:, s, :], in0=ring[:, s, :], scalar=1.0,
                                             in1=h_tok[:, 0, :], op0=ALU.mult, op1=ALU.mult,
                                             accum_out=act_u[:, 0, j:j + 1]).then_inc(u_used, 1)

            def row_first_tile(g):
                return lambda j: (ring[:, j % NG1, :], g_landed[j % NG1], 16 * (8 * g + 4 + j // NG1 + 1))

            def row_first_group(j):
                s, turn = j % NG, j // NG + 1
                if j < NG1 or j >= NG + NG1:
                    return extra[j % NG1], extra_landed[j % NG1], 16 * turn
                return ring[:, s, :], g_landed[s], 16 * (8 * HEADS + 1) if s < NG1 else 16

            def row_later(g):
                def row(j):
                    s, turn = j % NG, 2 * (g - HEADS) + j // NG
                    return ring[:, s, :], g_landed[s], 16 * turn + (16 * 8 * HEADS if s < NG1 else 0)
                return row

            stage_first(0, 0, staged)
            with dve.Fori(0, HEADS) as g:
                stage_first(g, 1, staged_v)
                products_u(g, range(K // 2))
                choose(4 * g + 1)
                products_u(g, range(K // 2, K))
                stage_first(g + 1, 0, staged)
                choose(4 * g + 2)
                weigh(g)
                add_rows(g, acc0, row_first_tile(g), range(K // 2))
                choose(4 * g + 3)
                add_rows(g, acc0, row_first_tile(g), range(K // 2, K))
                choose(4 * g + 4)
            dve.tensor_copy(vidx_st[:, 0, :], vidx[:, HEADS * K:(HEADS + 1) * K])
            dve.drain().then_inc(staged, 1)
            dve.wait_ge(rows2_landed, 16)
            second_ln(0, acc0)

            def group(g, par, acc, row):
                stage(g + 1, 1 - par)
                weigh(g)
                add_rows(g, acc, row)

            def group_pairs(t, first, acc):
                with dve.Fori(first, HEADS // 2) as hp:
                    for par in range(2):
                        g = t * HEADS + 2 * hp + par
                        group(g, par, acc, row_later(g))

            acc1 = h_tok[:, 1, :]
            dve.tensor_scalar(acc1, acc1, ALPHA, None, ALU.mult)
            dve.drain()
            group(HEADS, 0, acc1, row_first_group)
            group(HEADS + 1, 1, acc1, row_later(HEADS + 1))
            group_pairs(1, 1, acc1)
            second_ln(1, acc1)
            with dve.Fori(2, TT) as t:
                acc = h_tok[:, bass.ds(t, 1), :].rearrange("p a d -> p (a d)")
                dve.tensor_scalar(acc, acc, ALPHA, None, ALU.mult)
                dve.drain()
                group_pairs(t, 0, acc)
                second_ln(t, acc)

        @block.tensor
        def _(pe):
            def stationary_unit(dst, u, ready=None):
                for half in range(2):
                    pe.wait_ge(halves_split, 2 * u + half + 1)
                    for k in range(8):
                        kt = 8 * half + k
                        if ready is not None:
                            pe.wait_ge(ready, kt + 1)
                        wh, wl = (part[:, half, k * P:(k + 1) * P] for part in (w_high, w_low))
                        pe.matmul(dst, wh, src_high[:, kt, :], start=(kt == 0), stop=False)
                        pe.matmul(dst, wh, src_low[:, kt, :], start=False, stop=False)
                        mm = pe.matmul(dst, wl, src_high[:, kt, :], start=False, stop=(kt == KT - 1))
                    mm.then_inc(halves_done, 1)

            def moving_group(c, order, first_unit, done, freed, ready=None):
                for q in range(4):
                    for half in range(2):
                        last = q == 3 and half == 1
                        pe.wait_ge(halves_split, 2 * (first_unit + 4 * c + q) + half + 1)
                        for k in range(2):
                            n = 4 * q + 2 * half + k
                            if ready is not None:
                                ready(n)
                            wh, wl = (part[:, half, k * COLS:(k + 1) * COLS] for part in (w_high, w_low))
                            for t in range(TT):
                                if n == 0 and freed is not None:
                                    pe.wait_ge(*freed(t))
                                sh, sl = (part[:, order[n], P * t:P * t + P] for part in (src_high, src_low))
                                pe.matmul(bank(t), sh, wh, start=(n == 0), stop=False)
                                pe.matmul(bank(t), sh, wl, start=False, stop=False)
                                mm = pe.matmul(bank(t), sl, wh, start=False, stop=(n == KT - 1))
                                if n == KT - 1:
                                    mm.then_inc(done, 1)
                        if not last:
                            mm.then_inc(halves_done, 1)
                        else:
                            pe.drain().then_inc(halves_done, 1)

            natural = list(range(KT))
            moving_group(0, natural, U_VG, vg_bank_done, None,
                         lambda n: pe.wait_ge(x_split, n // 2 + 1))
            with pe.Fori(1, 4) as c:
                moving_group(c, natural, U_VG, vg_bank_done,
                             lambda t: (vg_bank_free, TT * (c - 1) + t + 1))

            def lru_gates(g, p):
                pe.wait_ge(gate_landed[p], 8 * (g - p) + 16)
                pe.wait_ge(conv_done, g + 1)
                pe.matmul(bank(4 * p + 2), wgate[:, p, 0, :], xc[p], start=True, stop=True)
                pe.matmul(bank(4 * p + 3), wgate[:, p, 1, :], xc[p], start=True, stop=True).then_inc(gates_mm, 1)

            def lru_block(g, p):
                stationary_unit(bank(4 * p), U_LRU + 2 * g)

            def lru_block_gr(g, p, first):
                if not first:
                    pe.wait_ge(lru_act, 2 * (g - 1))
                stationary_unit(bank(4 * p + 1), U_LRU + 2 * g + 1)

            pe.wait_ge(vg_bank_free, 4 * TT)
            lru_block(0, 0)
            lru_block_gr(0, 0, True)
            lru_block(1, 1)
            lru_gates(0, 0)
            lru_block_gr(1, 1, True)
            with pe.Fori(1, HEADS // 2) as r:
                for p in range(2):
                    g = 2 * r + p
                    lru_block(g, p)
                    lru_gates(g - 1, 1 - p)
                    lru_block_gr(g, p, False)
            lru_gates(HEADS - 1, 1)

            def head_q(h, p, first):
                if not first:
                    pe.wait_ge(rot_q, h - 1)
                stationary_unit(bank(p), U_QK + 2 * h)

            def head_k(h, p, first):
                if not first:
                    pe.wait_ge(rot_k, h - 1)
                stationary_unit(bank(2 + p), U_QK + 2 * h + 1)

            def scores(h, p, first=False):
                pe.wait_ge(rot_q, h + 1)
                pe.wait_ge(rot_k, h + 1)
                for i in range(TT):
                    if not (first and i < 2):
                        pe.wait_ge(masked, TT * h + i - 1)
                    pe.matmul(bank(4 + i % 2)[:, 0:SEQ - P * i], kT[p][:, P * i:P * i + P],
                              qT[p][:, P * i:SEQ], start=True, stop=True).then_inc(scores_mm, 1)

            def outputs(h, p):
                pe.wait_ge(masked, TT * (h + 1))
                for c in range(TT):
                    for i in range(c + 1):
                        mm = pe.matmul(bank(6 + p)[:, P * c:P * c + P], probs[:, i, P * (c - i):P * (c - i + 1)],
                                       vg[:, i, bass.ds(P * h, P)], start=(i == 0), stop=(i == c))
                mm.then_inc(o_mm, 1)

            head_q(0, 0, True)
            pe.wait_ge(lru_act, 2 * (HEADS - 1))
            head_k(0, 0, True)
            head_q(1, 1, True)
            pe.wait_ge(lru_act, 2 * HEADS)
            scores(0, 0, True)
            head_k(1, 1, True)
            outputs(0, 0)
            with pe.Fori(1, HEADS // 2) as r:
                for p in range(2):
                    h = 2 * r + p
                    head_q(h, p, False)
                    scores(h - 1, 1 - p)
                    head_k(h, p, False)
                    outputs(h - 1, 1 - p)
            scores(HEADS - 1, 1)
            outputs(HEADS - 1, 1)

            def mix_tile(n):
                if n < HEADS:
                    pe.wait_ge(ret_done, n + 1)
                    if n >= 3:
                        pe.wait_ge(mix_split, HEADS + n - 2)
                    for t in range(TT):
                        mm = pe.transpose(bank(4 + n % 3)[:, P * t:P * t + P],
                                          vg[:, t, 1024 + P * n:1024 + P * n + P], ident[:, :])
                    mm.then_inc(ret_tr, 1)
                pe.wait_ge(mix_split, n + 1)

            mix_order = list(range(HEADS, KT)) + list(range(HEADS))
            moving_group(0, mix_order, U_OUT, mix_bank_done, None, mix_tile)
            with pe.Fori(1, 4) as c:
                moving_group(c, mix_order, U_OUT, mix_bank_done,
                             lambda t: (mix_added, TT * (c - 1) + t + 1))

            for k in range(KT):
                if k % 4 == 0:
                    pe.wait_ge(ln1_normed, TT * (k // 4 + 1))
                if k >= 8:
                    pe.wait_ge(h_copied, k - 7)
                for t in range(TT):
                    mm = pe.transpose(bank(k % 8)[:, P * t:P * t + P], h_tok[:, t, P * k:P * k + P],
                                      ident[:, :])
                mm.then_inc(h_tr, 1)

            def queries(n, p, first):
                if not first:
                    pe.wait_ge(qp_copied, n - 1)
                stationary_unit(bank(p), U_PQ + n)

            def key_scores(n, p, first):
                pe.wait_ge(qp_copied, n + 1)
                if not first:
                    pe.wait_ge(keys_copied, 2 * (n - 1))
                for t in range(TT):
                    mm = pe.matmul(bank(2 + p)[:, P * t:P * t + P], qpT[p][:, P * t:P * t + P],
                                   sub_sb[:, bass.ds(n, 1), :].rearrange("p a k -> p (a k)"),
                                   start=True, stop=True)
                mm.then_inc(key_mm, 1)

            for n in range(4):
                if n == 0:
                    pe.wait_ge(h_copied, 9)
                    stationary_unit(bank(0), U_PQ, h_split)
                else:
                    queries(n, n % 2, n < 2)
                if n == 1:
                    pe.wait_ge(sub_landed, 16)
                if n:
                    key_scores(n - 1, (n - 1) % 2, n < 3)
            with pe.Fori(1, 4) as r:
                for m in range(4):
                    n = 4 * r + m
                    queries(n, m % 2, False)
                    key_scores(n - 1, (m - 1) % 2, False)
            key_scores(15, 1, False)

            def chunk_products(c, b, first):
                for q in range(4):
                    pe.wait_ge(w_landed[q], 16 * (U_PEER // NW + c + 1))
                    ut = wslot[q].rearrange("p (k n) -> p k n", n=COLS)
                    for t in range(DENSE):
                        if q == 0:
                            pe.wait_ge(score_copied, DENSE * c + t + 1)
                        for k in range(4):
                            if first and t == 0:
                                pe.wait_ge(h_whole, 4 * q + k + 1)
                            mm = pe.matmul(bank(DENSE * b + t), hT[:, 4 * q + k, P * (t + 1):P * (t + 2)],
                                           ut[:, k, :], start=(q == 0 and k == 0), stop=(q == 3 and k == 3))
                        if q == 3:
                            mm.then_inc(score_bank_done, 1)
                    if q < 3:
                        mm.then_inc(halves_done, 2)
                    else:
                        pe.drain().then_inc(halves_done, 2)

            pe.wait_ge(keys_copied, 4 * HEADS)
            chunk_products(0, 0, True)
            chunk_products(1, 1, False)
            with pe.Fori(1, CHUNKS // 2) as r:
                for b in range(2):
                    chunk_products(2 * r + b, b, False)


_OUT_SHAPE = (1, SEQ, D)


def _constants():
    import numpy as np
    half = P // 2
    freq = (10000.0 ** (-(np.arange(half, dtype=np.float32)) / np.float32(half))).astype(np.float32)
    m = np.arange(P)[:, None]
    c = np.arange(SEQ)[None, :]
    same, later = c // CHUNK == m // CHUNK, c // CHUNK > m // CHUNK
    gap = np.where(same, np.abs(c - m), c - m).astype(np.float64)
    decay = np.zeros((P, HEADS, SEQ), np.float32)
    for h in range(HEADS):
        gamma = 1.0 - 2.0 ** (-5.0 - h)
        decay[:, h, :] = np.where(same | later, gamma ** np.maximum(gap, 0.0), 0.0) * P ** -0.5
    return {
        "ident_c": np.eye(P, dtype=np.float32),
        "decay_c": decay,
        "freq_c": np.concatenate([freq, freq])[:, None],
        "base_c": ((np.clip(np.arange(TT * HEADS + 1) // HEADS - 1, 0, DENSE - 1) * P)[None, :]
                   + np.arange(P)[:, None]).astype(np.float32) * EXPERTS,
        "iota_c": np.tile(np.arange(K, dtype=np.float32), (P, 1)),
    }


def _stationary(wt, columns):
    return wt[:, columns].reshape(KT, P, -1, P).transpose(2, 1, 0, 3).reshape(-1, P, KT * P)


def _moving(wt, order):
    t = wt.reshape(KT, P, -1, COLS)[order]
    return t.reshape(4, 4, P, -1, COLS).transpose(3, 0, 2, 1, 4).reshape(-1, P, 4 * COLS)


def kernel(x, positions, w_in, w_out, conv_w, conv_b, w_ra, b_ra, w_ri, b_ri, lru_lambda,
           ln1_g, ln1_b, w_pq, sub_keys, peer_u, peer_v, ln2_g, ln2_b):
    import numpy as np
    import concourse.bacc as bacc
    from concourse.bass_utils import run_bass_kernel_spmd

    x, w_in, w_out, w_pq = np.asarray(x)[0], np.asarray(w_in)[0], np.asarray(w_out)[0], np.asarray(w_pq)[0]

    def turns(a, b):
        return np.concatenate([np.r_[s + P * n:s + P * n + P] for n in range(HEADS) for s in (a, b)])

    natural = list(range(KT))
    units = np.concatenate([
        _moving(w_in[:, 2048:4096], natural),
        _stationary(w_in, turns(4096, 5120)),
        _stationary(w_in, turns(0, 1024)),
        _moving(w_out, natural[HEADS:] + natural[:HEADS]),
        _stationary(w_pq, slice(None)),
    ])
    per_channel = [np.asarray(conv_w)[0][n] for n in range(4)] + [
        np.asarray(a)[0] for a in (conv_b, b_ra, b_ri, lru_lambda)]
    arrays = {
        "x_tok": np.ascontiguousarray(x.reshape(TT, P, D).transpose(1, 0, 2)),
        "x_t": np.ascontiguousarray(x.T.reshape(4, 4, P, SEQ).transpose(0, 2, 1, 3)),
        "positions": np.ascontiguousarray(positions),
        "w_units": np.ascontiguousarray(units),
        "u_units": np.ascontiguousarray(_moving(np.asarray(peer_u)[0].T, natural)),
        "gate_w": np.ascontiguousarray(np.stack([np.asarray(w_ra)[0], np.asarray(w_ri)[0]], 1)
                                       .transpose(0, 2, 1, 3)),
        "chan": np.ascontiguousarray(np.stack(per_channel).reshape(8, HEADS, P).transpose(2, 0, 1)),
        "sub_t": np.ascontiguousarray(np.asarray(sub_keys)[0].reshape(KT, NKEYS, P).transpose(2, 0, 1)),
        "ln1_t": np.ascontiguousarray(np.stack([np.asarray(ln1_g)[0], np.asarray(ln1_b)[0]])
                                      .reshape(2, KT, P).transpose(2, 0, 1)),
        "ln_rows": np.ascontiguousarray(np.concatenate([np.asarray(a) for a in (ln1_g, ln1_b, ln2_g, ln2_b)])),
        "peer_u": np.ascontiguousarray(np.asarray(peer_u)[0]),
        "peer_v": np.ascontiguousarray(np.asarray(peer_v)[0]),
        **_constants(),
    }
    nc = bacc.Bacc("TRN2", target_bir_lowering=False, num_devices=1)
    aps = {n: nc.dram_tensor(n, a.shape, mybir.dt.from_np(a.dtype), kind="ExternalInput").ap()
           for n, a in arrays.items()}
    out = nc.dram_tensor("out", _OUT_SHAPE, F32, kind="ExternalOutput").ap()
    build(nc, out=out, **aps)
    result = run_bass_kernel_spmd(nc, [arrays], core_ids=[0])
    return result.results[0]["out"]
```
